# Optimizing a Trainium2 kernel written in Bass

```python
import jax
import jax.numpy as jnp
from jax import lax
import numpy as np

"""Hybrid decoder layer with Hymba-style parallel head groups.

Each layer computes
  h  = x + W_out [ SWA-GQA-sink(ALiBi) | MLA(decoupled rope) | memory cross-attn ](RMSNorm(x))
  out = h + SwiGLU(RMSNorm(h))
All three head groups read one combined input projection of the same normalised input.
Inputs : x (BATCH, SEQ, D_MODEL) f32, mem (BATCH, 256, D_MODEL) f32, positions (BATCH, SEQ) int32,
         plus per-layer parameters stacked on a leading DEPTH axis.
Output : (BATCH, SEQ, D_MODEL).
"""

D_MODEL = 2048
BATCH = 1
SEQ = 512
DEPTH = 1

MEM_LEN = 256
BLOCK = 128
EPS = 1e-6
NEG_INF = -1e30

SWA_Q_HEADS = 16
SWA_KV_HEADS = 2
SWA_HEAD_DIM = 64
WINDOW = 128

MLA_HEADS = 4
MLA_Q_RANK = 512
MLA_KV_RANK = 512
MLA_NOPE_DIM = 128
MLA_ROPE_DIM = 64
MLA_V_DIM = 128
ROPE_THETA = 10000.0

MEM_HEADS = 4
MEM_HEAD_DIM = 128

MIX_WIDTH = SWA_Q_HEADS * SWA_HEAD_DIM + MLA_HEADS * MLA_V_DIM + MEM_HEADS * MEM_HEAD_DIM
IN_SIZES = (SWA_Q_HEADS * SWA_HEAD_DIM, SWA_KV_HEADS * SWA_HEAD_DIM, SWA_KV_HEADS * SWA_HEAD_DIM,
            MLA_Q_RANK, MLA_KV_RANK, MLA_ROPE_DIM, MEM_HEADS * MEM_HEAD_DIM)
IN_WIDTH = sum(IN_SIZES)
IN_SPLITS = tuple(int(v) for v in np.cumsum(IN_SIZES)[:-1])

D_FF = ((8 * D_MODEL + 3 * 256 - 1) // (3 * 256)) * 256

kernel_name = "hymba_swa_sink_mla_memory_swiglu"

def rms_norm(x, g):
    xf = x.astype(jnp.float32)
    y = xf * lax.rsqrt(jnp.mean(xf * xf, axis=-1, keepdims=True) + EPS)
    return (y * g.astype(jnp.float32)).astype(x.dtype)

def alibi_slopes(n):
    return 2.0 ** (-8.0 * jnp.arange(1, n + 1, dtype=jnp.float32) / n)

def apply_rope(x, cos, sin):
    x1, x2 = jnp.split(x.astype(jnp.float32), 2, axis=-1)
    return jnp.concatenate([x1 * cos - x2 * sin, x1 * sin + x2 * cos], axis=-1).astype(x.dtype)

def swa_sink_attention(q, k, v, pos, sinks):
    b, s, _, d = q.shape
    nb = s // BLOCK
    g = SWA_Q_HEADS // SWA_KV_HEADS
    qb = q.reshape(b, nb, BLOCK, SWA_KV_HEADS, g, d)

    def with_prev(t):
        tb = t.reshape((b, nb, BLOCK) + t.shape[2:])
        prev = jnp.concatenate([jnp.zeros_like(tb[:, :1]), tb[:, :-1]], axis=1)
        return jnp.concatenate([prev, tb], axis=2)

    kb, vb, pk = with_prev(k), with_prev(v), with_prev(pos)
    pq = pos.reshape(b, nb, BLOCK)
    scores = jnp.einsum('bnqhgd,bnkhd->bnhgqk', qb, kb,
                        preferred_element_type=jnp.float32) * (d ** -0.5)
    dist = jnp.abs(pq[:, :, :, None] - pk[:, :, None, :]).astype(jnp.float32)
    slopes = alibi_slopes(SWA_Q_HEADS).reshape(SWA_KV_HEADS, g)
    scores = scores - slopes[None, None, :, :, None, None] * dist[:, :, None, None]
    qi = jnp.arange(BLOCK)[:, None] + BLOCK
    ki = jnp.arange(2 * BLOCK)[None, :]
    band = (ki <= qi) & (qi - ki < WINDOW)
    not_first = jnp.arange(nb)[:, None, None] > 0
    valid = band[None] & (not_first | (ki >= BLOCK)[None])
    scores = jnp.where(valid[None, :, None, None], scores, NEG_INF)
    sink = sinks.astype(jnp.float32).reshape(SWA_KV_HEADS, g)[None, None, :, :, None, None]
    m = jnp.maximum(jnp.max(scores, axis=-1, keepdims=True), sink)
    p = jnp.exp(scores - m)
    p = p / (jnp.sum(p, axis=-1, keepdims=True) + jnp.exp(sink - m))
    out = jnp.einsum('bnhgqk,bnkhd->bnqhgd', p.astype(v.dtype), vb)
    return out.reshape(b, s, SWA_Q_HEADS * d)

def mla_causal_attention(q_nope, q_rope, k_nope, k_rope, v):
    b, s, h, _ = q_nope.shape
    nb = s // BLOCK
    scale = (MLA_NOPE_DIM + MLA_ROPE_DIM) ** -0.5
    k_idx = jnp.arange(s)

    def to_blocks(t):
        return jnp.moveaxis(t.reshape((b, nb, BLOCK) + t.shape[2:]), 1, 0)

    def one_block(args):
        qn, qr, i = args
        sc = (jnp.einsum('bqhd,bkhd->bhqk', qn, k_nope, preferred_element_type=jnp.float32)
              + jnp.einsum('bqhd,bkd->bhqk', qr, k_rope, preferred_element_type=jnp.float32)) * scale
        q_idx = i * BLOCK + jnp.arange(BLOCK)
        sc = jnp.where(k_idx[None, :] <= q_idx[:, None], sc, NEG_INF)
        p = jax.nn.softmax(sc, axis=-1).astype(v.dtype)
        return jnp.einsum('bhqk,bkhd->bqhd', p, v)

    out = lax.map(one_block, (to_blocks(q_nope), to_blocks(q_rope), jnp.arange(nb)))
    return jnp.moveaxis(out, 0, 1).reshape(b, s, h * MLA_V_DIM)

def memory_cross_attention(q, k, v):
    b, s, h, d = q.shape
    sc = jnp.einsum('bshd,bmhd->bhsm', q, k, preferred_element_type=jnp.float32) * (d ** -0.5)
    p = jax.nn.softmax(sc, axis=-1).astype(v.dtype)
    return jnp.einsum('bhsm,bmhd->bshd', p, v).reshape(b, s, h * d)

def setup_inputs(seed: int = 0) -> dict:
    key = jax.random.key(seed)
    ks = iter(jax.random.split(key, 32))

    def nrm(shape, fan_in):
        return jax.random.normal(next(ks), shape, jnp.float32) * (fan_in ** -0.5)

    def gain(n):
        return 1.0 + 0.02 * jax.random.normal(next(ks), (DEPTH, n), jnp.float32)

    x = jax.random.normal(next(ks), (BATCH, SEQ, D_MODEL), jnp.float32)
    mem = jax.random.normal(next(ks), (BATCH, MEM_LEN, D_MODEL), jnp.float32)
    offsets = jax.random.randint(next(ks), (BATCH, 1), 0, 1024, dtype=jnp.int32)
    positions = offsets + jnp.arange(SEQ, dtype=jnp.int32)[None, :]
    return {
        "x": x,
        "mem": mem,
        "positions": positions,
        "attn_norm_g": gain(D_MODEL),
        "w_in": nrm((DEPTH, D_MODEL, IN_WIDTH), D_MODEL),
        "swa_q_norm_g": gain(SWA_HEAD_DIM),
        "swa_k_norm_g": gain(SWA_HEAD_DIM),
        "swa_sinks": 0.5 * jax.random.normal(next(ks), (DEPTH, SWA_Q_HEADS), jnp.float32),
        "mla_cq_norm_g": gain(MLA_Q_RANK),
        "mla_ckv_norm_g": gain(MLA_KV_RANK),
        "w_uq": nrm((DEPTH, MLA_Q_RANK, MLA_HEADS * (MLA_NOPE_DIM + MLA_ROPE_DIM)), MLA_Q_RANK),
        "w_ukv": nrm((DEPTH, MLA_KV_RANK, MLA_HEADS * (MLA_NOPE_DIM + MLA_V_DIM)), MLA_KV_RANK),
        "mla_qn_norm_g": gain(MLA_NOPE_DIM),
        "mla_qr_norm_g": gain(MLA_ROPE_DIM),
        "mla_kn_norm_g": gain(MLA_NOPE_DIM),
        "mla_kr_norm_g": gain(MLA_ROPE_DIM),
        "mem_norm_g": gain(D_MODEL),
        "w_mem_kv": nrm((DEPTH, D_MODEL, 2 * MEM_HEADS * MEM_HEAD_DIM), D_MODEL),
        "mem_q_norm_g": gain(MEM_HEAD_DIM),
        "mem_k_norm_g": gain(MEM_HEAD_DIM),
        "w_out": nrm((DEPTH, MIX_WIDTH, D_MODEL), MIX_WIDTH),
        "ffn_norm_g": gain(D_MODEL),
        "w_gate": nrm((DEPTH, D_MODEL, D_FF), D_MODEL),
        "w_up": nrm((DEPTH, D_MODEL, D_FF), D_MODEL),
        "w_down": nrm((DEPTH, D_FF, D_MODEL), D_FF),
    }

def reference(x, mem, positions, attn_norm_g, w_in, swa_q_norm_g, swa_k_norm_g, swa_sinks,
              mla_cq_norm_g, mla_ckv_norm_g, w_uq, w_ukv, mla_qn_norm_g, mla_qr_norm_g,
              mla_kn_norm_g, mla_kr_norm_g, mem_norm_g, w_mem_kv, mem_q_norm_g, mem_k_norm_g,
              w_out, ffn_norm_g, w_gate, w_up, w_down):
    b, s, _ = x.shape
    m_len = mem.shape[1]
    inv_freq = ROPE_THETA ** (-jnp.arange(0, MLA_ROPE_DIM, 2, dtype=jnp.float32) / MLA_ROPE_DIM)
    ang = positions.astype(jnp.float32)[..., None] * inv_freq
    cos, sin = jnp.cos(ang), jnp.sin(ang)
    h = x
    for l in range(DEPTH):
        hn = rms_norm(h, attn_norm_g[l])
        proj = hn @ w_in[l]
        q_a, k_a, v_a, c_q, c_kv, k_r, q_m = jnp.split(proj, IN_SPLITS, axis=-1)

        q_a = rms_norm(q_a.reshape(b, s, SWA_Q_HEADS, SWA_HEAD_DIM), swa_q_norm_g[l])
        k_a = rms_norm(k_a.reshape(b, s, SWA_KV_HEADS, SWA_HEAD_DIM), swa_k_norm_g[l])
        v_a = v_a.reshape(b, s, SWA_KV_HEADS, SWA_HEAD_DIM)
        y_a = swa_sink_attention(q_a, k_a, v_a, positions, swa_sinks[l])

        q_b = (rms_norm(c_q, mla_cq_norm_g[l]) @ w_uq[l]).reshape(
            b, s, MLA_HEADS, MLA_NOPE_DIM + MLA_ROPE_DIM)
        kv_b = (rms_norm(c_kv, mla_ckv_norm_g[l]) @ w_ukv[l]).reshape(
            b, s, MLA_HEADS, MLA_NOPE_DIM + MLA_V_DIM)
        q_nope = rms_norm(q_b[..., :MLA_NOPE_DIM], mla_qn_norm_g[l])
        q_rope = apply_rope(rms_norm(q_b[..., MLA_NOPE_DIM:], mla_qr_norm_g[l]),
                            cos[:, :, None], sin[:, :, None])
        k_nope = rms_norm(kv_b[..., :MLA_NOPE_DIM], mla_kn_norm_g[l])
        v_b = kv_b[..., MLA_NOPE_DIM:]
        k_rope = apply_rope(rms_norm(k_r, mla_kr_norm_g[l]), cos, sin)
        y_b = mla_causal_attention(q_nope, q_rope, k_nope, k_rope, v_b)

        q_m = rms_norm(q_m.reshape(b, s, MEM_HEADS, MEM_HEAD_DIM), mem_q_norm_g[l])
        kv_m = (rms_norm(mem, mem_norm_g[l]) @ w_mem_kv[l]).reshape(
            b, m_len, 2, MEM_HEADS, MEM_HEAD_DIM)
        k_m = rms_norm(kv_m[:, :, 0], mem_k_norm_g[l])
        v_m = kv_m[:, :, 1]
        y_m = memory_cross_attention(q_m, k_m, v_m)

        h = h + jnp.concatenate([y_a, y_b, y_m], axis=-1) @ w_out[l]

        fn = rms_norm(h, ffn_norm_g[l])
        h = h + (jax.nn.silu(fn @ w_gate[l]) * (fn @ w_up[l])) @ w_down[l]
    return h


_drawn_inputs = setup_inputs


def setup_inputs(seed=0):
    import zlib

    import numpy as np

    out = dict(_drawn_inputs(seed))
    spreads = {}
    factors = {'attn_norm_g': 7.622,
     'swa_q_norm_g': 8.0,
     'swa_k_norm_g': 8.0,
     'swa_sinks': 57.272,
     'mla_cq_norm_g': 8.0,
     'mla_ckv_norm_g': 8.0,
     'mla_qn_norm_g': 8.0,
     'mla_qr_norm_g': 8.0,
     'mla_kn_norm_g': 8.0,
     'mla_kr_norm_g': 8.0,
     'mem_norm_g': 8.0,
     'mem_q_norm_g': 8.0,
     'mem_k_norm_g': 8.0,
     'ffn_norm_g': 3.82}
    for name, (base, spread) in spreads.items():
        noise = np.random.default_rng([zlib.crc32(name.encode()), seed]).standard_normal(out[name].shape)
        drawn = base * np.exp(spread * noise) if base else spread * noise
        out[name] = jnp.asarray(drawn.astype(out[name].dtype))
    for name, factor in factors.items():
        out[name] = (out[name] * factor).astype(out[name].dtype)
    return out
```

```python
from contextlib import ExitStack

import numpy as np

import concourse.bass as bass
from concourse import mybir

ALU = mybir.AluOpType
ACT = mybir.ActivationFunctionType
AX = mybir.AxisListType
F32 = mybir.dt.float32
F32R = mybir.dt.float32r
I32 = mybir.dt.int32

P = 128
D = 2048
S = 512
MEM = 256
EPS = 1e-6
HA, GA, DA = 16, 2, 64
HB, NOPE, ROPE, RANK = 4, 128, 64, 512
HM = 4
DFF = ((8 * D + 3 * 256 - 1) // (3 * 256)) * 256
KC = D // P
NB = S // P
FT = DFF // P
FG = 4
FGT = FT // FG
SUB = 8
FILL = 1e30

IN_TILES = (["k_a", "v_a"] + [f"q_a{i}" for i in range(8)] + [f"c_q{i}" for i in range(4)]
            + [f"c_kv{i}" for i in range(4)] + ["k_r"] + [f"q_m{i}" for i in range(4)])
N_IN = len(IN_TILES)

SLOTS = []
for _i, _half in [(0, 0), (1, 0), (0, 1), (1, 1)] + [(t, half) for t in range(2, N_IN) for half in range(2)]:
    SLOTS.append(("in", (_i, _half), SUB * (ROPE if IN_TILES[_i] == "k_r" else P)))
for _i in range(HM):
    for _half in range(2):
        SLOTS.append(("mem_k", (_i, _half), SUB * P))
for _i in range(KC // 2):
    SLOTS.append(("mem_v", _i, SUB * P))
for _i in range(3):
    SLOTS.append(("uq", _i, SUB * P))
for _i in range(2):
    SLOTS.append(("uk", _i, SUB * P))
for _i in range(2):
    SLOTS.append(("uv", _i, SUB * P))
for _i in range(KC):
    SLOTS.append(("out_a", _i, SUB * P))
for _i in range(KC):
    SLOTS.append(("out_b", _i, SUB * P))
NS = len(SLOTS)

SLOTS_IN = 2 * N_IN
SLOTS_MEM = SLOTS_IN + 2 * HM + KC // 2
SLOTS_UV = SLOTS_MEM + 7


def make_ring():
    place, before, last = [], [], {}
    for i in range(NS):
        n = 3 if SLOTS_IN + 4 <= i < SLOTS_UV else 2
        free = [r for r in range(n) if r not in place[len(place) - n + 1:]] if i else [0]
        place.append(min(free, key=lambda r: last.get(r, -1)))
        before.append(last.get(place[-1]))
        last[place[-1]] = i
    return place, before


PLACE, SLOT_BEFORE = make_ring()
USE = [sum(q == PLACE[i] for q in PLACE[:i + 1]) for i in range(NS)]
THIRD = PLACE.index(2)

GROUPS = {}


def _group(name):
    GROUPS[name] = len(GROUPS)


for _n in IN_TILES:
    _group(_n)
for _i in range(HM):
    _group(("mem_k", _i))
for _i in range(MEM // P):
    _group(("mem_v", _i))
for _i in range(6):
    _group(("uq", _i))
for _i in range(4):
    _group(("uk", _i))
for _i in range(8):
    _group(("uv", _i))
for _i in range(KC):
    _group(("out_a", _i))
for _i in range(KC):
    _group(("out_b", _i))
NGROUPS = len(GROUPS)

STEPS = [("swa", b, g, r) for r in range(2) for b in range(NB) for g in range(GA)]
STEPS += [("mla", h, q, 0) for h in range(HB) for q in range(NB)]
STEPS += [("mem", h, q, 0) for h in range(HM) for q in range(NB)]
N_SWA = 16
N_STEPS = len(STEPS)

G_ATT, G_FFN, G_MEM, G_QA, G_KA, G_CQ, G_CKV = 0, 16, 32, 48, 49, 50, 54
G_QN, G_KN, G_QR, G_KR, G_QM, G_KM, G_ALL = 58, 59, 60, 62, 64, 65, 66

TWO_PI = 2 * np.pi
C1 = 6.28125
C2 = float(np.float32(np.round((TWO_PI - C1) * 2 ** 20) / 2 ** 20))
C3 = float(np.float32(TWO_PI - C1 - C2))
MAGIC = 1.5 * 2 ** 23
LN_EXP_SET = "natural_log_exp_and_others"


def make_plan():
    plan = []
    late = []
    state = {"slot": 0, "split": 2}

    def next_splits(i):
        while state["split"] < NS:
            n = state["split"]
            if (SLOTS_IN + 1 if n == THIRD else SLOT_BEFORE[n]) > i:
                break
            plan.append(("split", n))
            state["split"] += 1

    def run_slot(before_split=(), after_split=()):
        i = state["slot"]
        state["slot"] += 1
        plan.append(("slot", i))
        plan.extend(before_split)
        next_splits(i)
        while late:
            plan.extend(late.pop(0))
        plan.extend(after_split)

    def norm(name, n=1):
        return [("ss", (name, k, n)) for k in range(n)] + [("rstd", name), ("apply", name)] + (
            [("rotate", name)] if name in ("k_r", "q_r") else [])

    pair = lambda *js: [("x_pair", j) for j in js]
    squares = lambda lo, hi: [("x_sq", c) for c in range(lo, hi)]
    plan.extend([("split", 0)] + pair(0, 1, 2) + [("split", 1)] + pair(3) + squares(0, 1))
    run_slot(pair(4) + squares(1, 3) + pair(5) + squares(3, 4))
    run_slot(pair(6, 7) + squares(4, 8), squares(8, 12))
    run_slot(squares(12, KC))
    run_slot()
    plan.extend([("ss", ("x", 0, 1)), ("rstd", "x"), ("evac", "k_a"), ("sq", ("k_a", 0)), ("evac", "v_a")])
    late.append(norm("k_a") + [("v_turn", 0), ("setup", 0)])
    step = None
    squared = iter(range(KC // 2))

    def mem_square():
        k = next(squared)
        plan.extend([("sq", ("mem", k)), ("sum", ("mem", k))])

    for name in IN_TILES[2:]:
        begun = step is not None and step < N_SWA
        run_slot([("p_norm", step)] if begun else [], [("values", step - 1)] if step else [])
        if name in ("q_a1", "q_a2", "q_a3", "q_a4"):
            mem_square()
        if name == "q_a5":
            plan.extend([("ss", ("mem", 0, 1)), ("rstd", "mem")])
        if name in ("q_a6", "q_a7"):
            plan.append(("mem_scale", 2 * (name == "q_a7")))
        last = name == IN_TILES[-1]
        if name in ("q_a1", "q_a2", "q_a3", "q_a4"):
            mem_square()
        if name in ("q_a6", "q_a7"):
            plan.append(("mem_scale", 1 + 2 * (name == "q_a7")))
        if last:
            plan.extend([("mem_split", j) for j in range(4)])
        run_slot()
        plan.append(("evac", name))
        if name[:2] == "c_":
            base, k = name[:-1], int(name[-1])
            plan.extend([("sq", (base, k)), ("sum", (base, k))])
            if k == 3:
                late.append([("ss", (base, 0, 1)), ("rstd", base), ("apply", base)])
        elif name == "k_r":
            late.append([("rep", 0), ("sq", (name, 0)), ("sq", (name, 1))] + norm(name, 2))
        else:
            plan.append(("sq", (name, 0)))
            late.append(norm(name))
        if name == "q_a4":
            step = 0
            plan.extend([("scores", 0), ("softmax", 0)])
        elif step is not None:
            plan.append(("turn", step))
            step += 1
            if step < N_SWA:
                plan.extend([("scores", step), ("softmax", step)])
        if name == "q_a0":
            plan.extend([("mem_load", 0), ("angles", 0)])
        if name == "q_a1":
            plan.append(("sines", 0))
    assert step == N_SWA
    for i in range(HM):
        run_slot([], [("c_split", 2 * i)] + ([("values", N_SWA - 1)] if i == 0 else []))
        run_slot([("evac", ("mem_k", i)), ("sq", (("mem_k", i), 0))], [("c_split", 2 * i + 1)])
        late.append(norm(("mem_k", i)))
    for i in range(KC // 2):
        run_slot([("evac", ("mem_v", 0)), ("evac", ("mem_v", 1))] if i == KC // 2 - 1 else [])
    def two_heads(kind, i, after):
        this = []
        for m in (2 * i, 2 * i + 1):
            this.append(("evac", (kind, m)))
            if m < 4:
                this.append(("sq", ((kind, m), 0)))
        run_slot(this, after)
        late.extend(norm((kind, m)) for m in (2 * i, 2 * i + 1) if m < 4)

    windows = [("window_split", k) for k in range(SUB)]
    two_heads("uq", 0, windows[0:1])
    plan.append(("x_again", 0))
    two_heads("uq", 1, windows[1:2])
    plan.append(("x_again", 1))
    two_heads("uq", 2, [("sq", ("q_r", 0)), ("sq", ("q_r", 1))] + windows[2:4])
    late.append(norm("q_r", 2))
    two_heads("uk", 0, windows[4:5])
    two_heads("uk", 1, windows[5:8])
    for i in range(2):
        run_slot([("evac", ("uv", m)) for m in range(4 * i, 4 * i + 4)])

    def later_piece(n):
        if N_SWA <= n - 1 < N_STEPS:
            plan.append(("p_norm", n - 1))
        if N_SWA <= n - 3 < N_STEPS:
            plan.append(("values", n - 3))
        if N_SWA <= n - 2 < N_STEPS:
            plan.append(("turn", n - 2))
        if n < N_STEPS:
            plan.extend([("scores", n), ("softmax", n)])

    n = N_SWA
    for m in range(KC):
        i = state["slot"]
        state["slot"] += 1
        plan.append(("slot_half", (i, 0)))
        later_piece(n)
        plan.append(("slot_half", (i, 1)))
        later_piece(n + 1)
        n += 2
        next_splits(i)
        plan.append(("evac", ("out_a", m)))
        if m in (2, 4):
            plan.append(("x_again", 1 + m // 2))
    for k in range(3):
        later_piece(n + k)
    for m in range(KC):
        run_slot()
        plan.extend([("evac", ("out_b", m)), ("h_tile", m)])
    plan.extend([("first_ff_splits", 0), ("ss", ("h", 0, 1)), ("rstd", "h")])
    assert state["slot"] == NS
    return plan


PLAN = make_plan()


def count(stage):
    return {i: n + 1 for n, i in enumerate(i for s, i in PLAN if s == stage)}


SQ_AT = count("sq")
SUM_AT = count("sum")
SS_AT = count("ss")
NORM_AT = count("rstd")
APPLY_AT = count("apply")
SECOND = {n for n in NORM_AT if n[0] in ("mem_k", "uq", "uk") and n[1] % 2 or n == "q_r"}


def norm_before(name, own):
    same = [n for n in NORM_AT if (n in SECOND) == (name in SECOND) and not (own and n in ("x", "mem", "h"))]
    same = [n for n in same if NORM_AT[n] < NORM_AT[name]]
    return same[-1] if same else None


SS_END = {}
for (_n, _k, _m), _c in SS_AT.items():
    SS_END[_n] = _c
SS_OF_SQ = {SQ_AT[(_n, _k)]: _c for (_n, _k, _m), _c in SS_AT.items()
            if (_n, _k) in SQ_AT and (_n, _k) not in SUM_AT}
SUM_OF_SQ = {SQ_AT[_i]: _c for _i, _c in SUM_AT.items()}


SUM_END = {_n: _c for (_n, _k), _c in SUM_AT.items()}


def group_ends():
    ends, parts = {}, 0
    for i, (kind, at_, _) in enumerate(SLOTS):
        if kind == "in" and at_[1]:
            ends[IN_TILES[at_[0]]] = (True, i + 1)
        elif kind == "mem_k" and at_[1]:
            ends[("mem_k", at_[0])] = (True, i + 1)
        elif kind == "mem_v" and at_ == KC // 2 - 1:
            parts += 1
            ends[("mem_v", 0)] = (False, parts)
            ends[("mem_v", 1)] = (True, i + 1)
        elif kind in ("uq", "uk", "uv"):
            n = 4 if kind == "uv" else 2
            for j in range(n):
                last = j == n - 1
                parts += not last
                ends[(kind, n * at_ + j)] = (last, i + 1 if last else parts)
        elif kind in ("out_a", "out_b"):
            ends[(kind, at_)] = (True, i + 1)
    return ends


GROUP_ENDS = group_ends()


def build_layer(nc, xT, memT, pos_rows, pos_cols, gains, sink_rows, inv_freq, w_in, w_kr, w_memk, w_memv,
                w_uq, w_uk, w_uv, w_outa, w_outb, w_gu, w_dn, outT):
    plan = PLAN
    bank_of = {n: g % 2 for n, g in GROUPS.items()}

    with ExitStack() as ctx:
        def sem(name):
            return ctx.enter_context(nc.semaphore(name))

        base = (nc.sbuf_base + 63) // 64 * 64
        KB = 1024
        H0 = base
        B0 = H0 + 32 * KB
        A0 = B0 + 64 * KB
        S0 = A0 + 64 * KB
        C0 = S0 + 24 * KB
        top = [0]

        def at(name, shape, off, dt=F32):
            t = nc.alloc_sbuf_tensor_at(name, shape, dt, offset=off)
            return t

        def bump(name, shape, dt=F32):
            n = 4
            for s_ in shape[1:]:
                n *= s_
            t = at(name, shape, C0 + top[0], dt)
            top[0] += (n + 31) // 32 * 32
            return t

        x_sb = at("x_sb", [P, KC, S], H0)
        mem_raw = at("mem_raw", [P, KC, MEM], H0)
        win_p = at("win_p", [P, 4, 2 * P], H0 + 16 * KB)
        win_pt = at("win_pt", [P, 2, 4 * P], H0 + 20 * KB)
        dist = at("dist", [P, NB, 2 * P], H0 + 24 * KB)
        cos = at("cos", [P, S], H0 + 28 * KB)
        sin = at("sin", [P, S], H0 + 30 * KB)
        ang = at("ang", [P, S], H0 + 16 * KB)
        turns = at("turns", [P, S], H0 + 18 * KB)
        h_sb = at("h_sb", [P, KC, S], H0)

        q_a = at("q_a", [P, 8, S], B0)
        x_sq = at("x_sq", [P, KC, S], B0)
        q_m = at("q_m", [P, HM, S], B0 + 16 * KB)
        q_b = at("q_b", [P, 4, S], B0 + 24 * KB)
        k_b = at("k_b", [P, 4, S], B0 + 32 * KB)
        k_rt = at("k_rt", [P, 2, S], B0 + 40 * KB)
        q_rt = at("q_rt", [P, 2, S], B0 + 44 * KB)
        v_b = at("v_b", [P, NB, HB * P], B0 + 48 * KB)
        k_m = at("k_m", [P, HM, MEM], B0 + 56 * KB)
        v_m = at("v_m", [P, 2, HM * P], B0 + 60 * KB)
        f_hi = at("f_hi", [P, KC, S], B0, F32R)
        f_lo = at("f_lo", [P, KC, S], B0 + 32 * KB, F32R)

        xg_hi = at("xg_hi", [P, KC, S], A0, F32R)
        xg_lo = at("xg_lo", [P, KC, S], A0 + 32 * KB, F32R)
        mem_hi = at("mem_hi", [P, KC, MEM], A0, F32R)
        mem_lo = at("mem_lo", [P, KC, MEM], A0 + 32 * KB, F32R)
        c_hi = at("c_hi", [P, 8, S], A0 + 16 * KB, F32R)
        c_lo = at("c_lo", [P, 8, S], A0 + 48 * KB, F32R)
        y_hi = at("y_hi", [P, KC, S], A0, F32R)
        y_lo = at("y_lo", [P, KC, S], A0 + 32 * KB, F32R)
        hid_hi = at("hid_hi", [P, FGT, S], A0, F32R)
        hid_lo = at("hid_lo", [P, FGT, S], A0 + FGT * 2 * KB, F32R)

        raw = [at(f"raw{r}", [P, SUB * P], S0 + r * 4 * KB) for r in range(2)]
        w_hi = [at(f"w_hi{r}", [P, SUB * P], S0 + (2 + r) * 4 * KB, F32R) for r in range(2)]
        w_lo = [at(f"w_lo{r}", [P, SUB * P], S0 + (4 + r) * 4 * KB, F32R) for r in range(2)]
        raw.append(at("raw2", [P, SUB * P], H0 + 16 * KB))
        w_hi.append(at("w_hi2", [P, SUB * P], H0 + 20 * KB, F32R))
        w_lo.append(at("w_lo2", [P, SUB * P], H0 + 24 * KB, F32R))
        F0 = A0 + 2 * FGT * 2 * KB
        fw_hi = [at(f"fw_hi{r}", [P, KC * P], F0 + (2 * r) * 8 * KB, F32R) for r in range(2)]
        fw_lo = [at(f"fw_lo{r}", [P, KC * P], F0 + (2 * r + 1) * 8 * KB, F32R) for r in range(2)]

        k_a = bump("k_a", [P, S])
        v_a = bump("v_a", [P, NB, P])
        tmp = bump("tmp", [P, S])
        pos_f = bump("pos_f", [P, S])
        free_top = top[0]
        top[0] = 8 * KB
        fraw = [at("fraw0", [P, KC * P], C0), at("fraw1", [P, KC * P], F0 + 32 * KB)]
        assert free_top <= 8 * KB
        ident = bump("ident", [P, P])
        ones = bump("ones", [P, P])
        blk64 = bump("blk64", [P, P])
        blk32 = bump("blk32", [P, P])
        rep = bump("rep", [ROPE, 2, P])
        causal = bump("causal", [P, S])
        gain = bump("gain", [P, G_ALL])
        small = bump("small", [P, 64])
        cst = bump("cst", [P, 2])
        sink = bump("sink", [P, HA])
        nsink = bump("nsink", [P, HA])
        pos_q = bump("pos_q", [P, NB])
        scr0 = top[0]
        rstd_x = bump("rstd_x", [P, S])
        sq = bump("sq", [P, 2, S])
        rstd = bump("rstd", [P, S])
        end0 = top[0]
        top[0] = scr0
        p_sb = bump("p_sb", [P, 2, S])
        pt_sb = bump("pt_sb", [P, 2, S])
        top[0] = scr0
        ssum = bump("ssum", [P, S])
        hsq = bump("hsq", [P, 2, S])
        rstd_h = bump("rstd_h", [P, S])
        gate_sb = at("gate_sb", [P, S], C0 + scr0)
        up_sb = at("up_sb", [P, S], C0 + scr0 + 2 * KB)
        silu_sb = at("silu_sb", [P, S], C0 + scr0 + 4 * KB)
        top[0] = end0
        xsum = bump("xsum", [P, S])
        xsum_odd = at("xsum_odd", [P, S], C0 + scr0 + 2 * KB)
        rstd_m = at("rstd_m", [P, MEM], B0 + 60 * KB)
        pos_i = at("pos_i", [P, S], B0 + 48 * KB, I32)
        pos_qi = bump("pos_qi", [P, NB], I32)
        assert C0 + top[0] <= nc.sbuf_usable_end, (C0 + top[0], nc.sbuf_usable_end)

        invf = cst[:, 0:1]
        eps = cst[:, 1:2]

        def rstd_buf(name):
            return rstd_x if name in SECOND else rstd

        def stat(a, k):
            o = 4 + 28 * (a % 2) + 4 * k
            return small[:, o:o + 4]


        def psum(name, n):
            return ctx.enter_context(nc.psum_tensor(name, [P, n, S], F32))

        acc = psum("acc", 2)
        sc_ps = psum("sc_ps", 2)
        pt_ps = psum("pt_ps", 2)
        pv_ps = psum("pv_ps", 1)
        ss_first = psum("ss_first", 1)

        def ss_bank(name):
            return sc_ps[:, 0] if name in SECOND else ss_first[:, 0]


        x_in = [sem(f"x_in{i}") for i in range(KC // 2)]
        xg_hi_done = sem("xg_hi_done")
        sum_done, rotated = sem("sum_done"), sem("rotated")
        gain_in, small_in, mem_in = sem("gain_in"), sem("small_in"), sem("mem_in")
        x_again_in = [sem(f"x_again_in{i}") for i in range(4)]
        raw_in = [sem(f"raw_in{r}") for r in range(3)]
        fraw_in = [sem(f"fraw_in{r}") for r in range(2)]
        out_sent = sem("out_sent")
        consts_made = sem("consts_made")
        hi_done, lo_done, slot_done, part_done = sem("hi_done"), sem("lo_done"), sem("slot_done"), sem("part_done")
        acc_free = sem("acc_free")
        xg_done, xsq_done, xsum_done, xodd_done = sem("xg_done"), sem("xsq_done"), sem("xsum_done"), sem("xodd_done")
        hsq_done, hsum_done = sem("hsq_done"), sem("hsum_done")
        sq_done, ss_done, ln_done, rstd_done, applied = (sem("sq_done"), sem("ss_done"), sem("ln_done"),
                                                         sem("rstd_done"), sem("applied"))
        rep_done, rep_copied, v_turned, v_copied = (sem("rep_done"), sem("rep_copied"), sem("v_turned"),
                                                    sem("v_copied"))
        dist_made, dist_masked, arg_made, sin_made, cos_made, nsink_made = (
            sem("dist_made"), sem("dist_masked"), sem("arg_made"), sem("sin_made"), sem("cos_made"),
            sem("nsink_made"))
        c_hi_done, c_split, mem_scaled, mem_hi_done, mem_split = (
            sem("c_hi_done"), sem("c_split"), sem("mem_scaled"), sem("mem_hi_done"), sem("mem_split"))
        win_hi_done, win_split, y_hi_done, y_split = (sem("win_hi_done"), sem("win_split"), sem("y_hi_done"),
                                                      sem("y_split"))
        scores_done, max_ready, exp_done, p_ready, turned, pt_ready, values_done, y_done = (
            sem("scores_done"), sem("max_ready"), sem("exp_done"), sem("p_ready"), sem("turned"), sem("pt_ready"),
            sem("values_done"), sem("y_done"))
        dve_step, pool_step = sem("dve_step"), sem("pool_step")
        h_scaled, h_split = sem("h_scaled"), sem("h_split")
        silu_done, hid_made, hid_hi_done, hid_split = (sem("silu_done"), sem("hid_made"), sem("hid_hi_done"),
                                                       sem("hid_split"))

        block = ctx.enter_context(nc.Block())

        def source(i):
            kind, at_, _ = SLOTS[i]
            if kind == "in":
                t, half = at_
                if IN_TILES[t] == "k_r":
                    return w_kr[half]
                return w_in[t - (t > IN_TILES.index("k_r")), half]
            if kind == "mem_k":
                return w_memk[at_[0], at_[1]]
            return {"mem_v": w_memv, "uq": w_uq, "uk": w_uk, "uv": w_uv, "out_a": w_outa, "out_b": w_outb}[kind][at_]

        def earlier(a):
            return a if a < N_SWA else max(N_SWA, a - 1)

        def ff_slot(g, t, r):
            return g * (2 * FGT + KC) + 2 * t + r

        PAIRS = FGT + KC // 2

        def ff_loops(engine, gate_up, down):
            def group(g, n_after):
                with engine.Fori(0, FGT - 1) as t:
                    gate_up(g, t, KC)
                gate_up(g, FGT - 1, FGT)
                with engine.Fori(0, KC // 2 - 1) as t:
                    down(g, t, FGT)
                down(g, KC // 2 - 1, n_after)

            with engine.Fori(0, FG - 1) as g:
                group(g, KC)
            group(FG - 1, 0)

        def key_blocks(a):
            kind, u, v, _ = STEPS[a]
            if kind == "swa":
                return [0, 1] if u > 0 else [1]
            return list(range(v + 1 if kind == "mla" else MEM // P))

        @block.sync
        def _(sp):
            def load_slot(i):
                if i == THIRD:
                    sp.wait_ge(values_done, N_SWA)
                else:
                    sp.wait_ge(hi_done, SLOT_BEFORE[i] + 1)
                    sp.wait_ge(lo_done, SLOT_BEFORE[i] + 1)
                sp.dma_start(raw[PLACE[i]][:, 0:SLOTS[i][2]], source(i)).then_inc(raw_in[PLACE[i]], 16)

            sp.dma_start(raw[0][:], source(0)).then_inc(raw_in[0], 16)
            for c in range(KC // 2):
                sp.dma_start(x_sb[:, 2 * c:2 * c + 2], xT[:, 2 * c:2 * c + 2]).then_inc(x_in[c], 16)
                if c == 0:
                    sp.dma_start(gain[:], gains).then_inc(gain_in, 16)
                if c == 2:
                    sp.dma_start(raw[1][:], source(1)).then_inc(raw_in[1], 16)
                if c == 5:
                    load_slot(2)
            for stage, i in plan:
                if stage == "split" and i > 2:
                    load_slot(i)
                    if i == 3:
                        sp.dma_start(pos_i[:], pos_rows).then_inc(small_in, 16)
                        sp.dma_start(pos_qi[:], pos_cols).then_inc(small_in, 16)
                        sp.dma_start(sink[:], sink_rows).then_inc(small_in, 16)
                        sp.dma_start(invf, inv_freq).then_inc(small_in, 16)
                elif stage == "mem_load":
                    sp.wait_ge(xg_done, KC)
                    sp.wait_ge(xsq_done, KC)
                    sp.dma_start(mem_raw[:], memT).then_inc(mem_in, 16)
                elif stage == "x_again":
                    if i < 2:
                        sp.wait_ge(mem_split, 4)
                    else:
                        sp.wait_ge(slot_done, SLOTS_UV)
                        sp.wait_ge(rotated, 2)
                    sp.dma_start(h_sb[:, 4 * i:4 * i + 4], xT[:, 4 * i:4 * i + 4]).then_inc(x_again_in[i], 16)

            def load(slot, r, src, n):
                sp.wait_ge(lo_done, slot + NS - 1)
                sp.dma_start(fraw[r][:, 0:n * P], src).then_inc(fraw_in[r], 16)

            def gate_up(g, first):
                with sp.Fori(first, FGT) as t:
                    for r in range(2):
                        load(ff_slot(g, t, r), r, w_gu[(g * FGT + t) * 2 + r], KC)

            def down(g):
                with sp.Fori(0, KC // 2) as t:
                    for r in range(2):
                        load(ff_slot(g, t + FGT, r), r, w_dn[g * KC + t * 2 + r], FGT)

            load(0, 0, w_gu[0], KC)
            sp.wait_ge(slot_done, NS)
            load(1, 1, w_gu[1], KC)
            gate_up(0, 1)
            down(0)
            with sp.Fori(1, FG) as g:
                gate_up(g, 0)
                down(g)

        @block.tensor
        def _(pe):
            mm = nc.tensor.matmul

            def three(out, hi, lo, x_hi, x_lo, start, stop):
                mm(out, hi, x_hi, start=start, stop=False)
                mm(out, hi, x_lo, start=False, stop=False)
                return mm(out, lo, x_hi, start=False, stop=stop)

            def open_group(name):
                g = GROUPS[name]
                if g >= 2:
                    pe.wait_ge(acc_free, g - 1)

            def slot(i, part=None):
                kind, at_, _ = SLOTS[i]
                hi, lo = w_hi[PLACE[i]], w_lo[PLACE[i]]
                if part != 1:
                    pe.wait_ge(hi_done, i + 1)
                    pe.wait_ge(lo_done, i + 1)
                if kind == "in":
                    t, half = at_
                    name = IN_TILES[t]
                    m = ROPE if name == "k_r" else P
                    if half == 0:
                        open_group(name)
                    for k in range(SUB):
                        c = half * SUB + k
                        if t == 0:
                            pe.wait_ge(xg_done, c + 1)
                        last = three(acc[0:m, bank_of[name]], hi[:, k * m:(k + 1) * m], lo[:, k * m:(k + 1) * m],
                                     xg_hi[:, c], xg_lo[:, c], c == 0, c == KC - 1)
                elif kind == "mem_k":
                    h, half = at_
                    name = (kind, h)
                    if half == 0:
                        open_group(name)
                    for k in range(SUB):
                        c = half * SUB + k
                        if h == 0 and c % 4 == 0:
                            pe.wait_ge(mem_split, c // 4 + 1)
                        last = three(acc[:, bank_of[name], 0:MEM], hi[:, k * P:(k + 1) * P], lo[:, k * P:(k + 1) * P],
                                     mem_hi[:, c], mem_lo[:, c], c == 0, c == KC - 1)
                elif kind == "mem_v":
                    for t in range(MEM // P):
                        name = (kind, t)
                        if at_ == 0:
                            open_group(name)
                        for k in range(2):
                            c = 2 * at_ + k
                            rows = slice(t * P, (t + 1) * P)
                            out = acc[:, bank_of[name]]
                            wh, wl = hi[:, k * S:(k + 1) * S], lo[:, k * S:(k + 1) * S]
                            mm(out, mem_hi[:, c, rows], wh, start=c == 0, stop=False)
                            mm(out, mem_hi[:, c, rows], wl, start=False, stop=False)
                            last = mm(out, mem_lo[:, c, rows], wh, start=False, stop=c == KC - 1)
                        if (at_, t) == (KC // 2 - 1, 0):
                            last.then_inc(part_done, 1)
                elif kind in ("uq", "uk"):
                    off = 0 if kind == "uq" else 4
                    for j in range(2):
                        name = (kind, 2 * at_ + j)
                        open_group(name)
                        if name == ("uq", 0):
                            pe.wait_ge(c_split, 8)
                        for c in range(4):
                            k = j * 4 + c
                            last = three(acc[:, bank_of[name]], hi[:, k * P:(k + 1) * P], lo[:, k * P:(k + 1) * P],
                                         c_hi[:, off + c], c_lo[:, off + c], c == 0, c == 3)
                        if j == 0:
                            last.then_inc(part_done, 1)
                elif kind == "uv":
                    for t in range(NB):
                        name = (kind, 4 * at_ + t)
                        open_group(name)
                        rows = slice(t * P, (t + 1) * P)
                        for c in range(4):
                            out = acc[:, bank_of[name], 0:2 * P]
                            wh, wl = hi[:, c * 2 * P:(c + 1) * 2 * P], lo[:, c * 2 * P:(c + 1) * 2 * P]
                            mm(out, c_hi[:, 4 + c, rows], wh, start=c == 0, stop=False)
                            mm(out, c_hi[:, 4 + c, rows], wl, start=False, stop=False)
                            last = mm(out, c_lo[:, 4 + c, rows], wh, start=False, stop=c == 3)
                        if t < NB - 1:
                            last.then_inc(part_done, 1)
                else:
                    off = 0 if kind == "out_a" else SUB
                    name = (kind, at_)
                    if part != 1:
                        open_group(name)
                    for k in range(SUB) if part is None else range(4 * part, 4 * part + 4):
                        if name == ("out_a", 0):
                            pe.wait_ge(win_split, k + 1)
                        if name == ("out_b", 0):
                            pe.wait_ge(y_split, k + 1)
                        last = three(acc[:, bank_of[name]], hi[:, k * P:(k + 1) * P], lo[:, k * P:(k + 1) * P],
                                     y_hi[:, off + k], y_lo[:, off + k], k == 0, k == SUB - 1)
                if part != 0:
                    last.then_inc(slot_done, 1)

            def sum_squares(name, k, n):
                if k == 0 and norm_before(name, False):
                    pe.wait_ge(rstd_done, NORM_AT[norm_before(name, False)])
                elif name in SECOND:
                    pe.wait_ge(p_ready, N_SWA)
                ss_ps = ss_bank(name)
                if name == "x":
                    pe.wait_ge(consts_made, 1)
                    pe.wait_ge(xsum_done, KC // 2)
                    pe.wait_ge(xodd_done, KC // 2)
                    src = xsum[:]
                    mm(ss_ps, ones[:], xsum_odd[:], start=True, stop=False)
                elif name == "h":
                    pe.wait_ge(hsum_done, KC)
                    src = ssum[:]
                elif (name, k) in SUM_AT:
                    pe.wait_ge(sum_done, SUM_END[name])
                    src = xsum[:]
                else:
                    pe.wait_ge(sq_done, SQ_AT[(name, k)])
                    src = sq[:, (SQ_AT[(name, k)] - 1) % 2]
                if name == "k_a" or (isinstance(name, str) and name.startswith("q_a")):
                    group = blk64
                elif name in ("k_r", "q_r"):
                    group = blk32
                else:
                    group = ones
                if name == "mem":
                    mm(ss_ps[:, 0:MEM], group[:], src[:, 0:MEM], start=True, stop=False)
                    mm(ss_ps[:, 0:MEM], group[:], src[:, MEM:], start=False, stop=True).then_inc(ss_done, 1)
                elif name[0] == "mem_k":
                    mm(ss_ps[:, 0:MEM], group[:], src[:, 0:MEM], start=True, stop=True).then_inc(ss_done, 1)
                else:
                    mm(ss_ps, group[:], src, start=k == 0 and name != "x", stop=k == n - 1).then_inc(ss_done, 1)

            def scores(a):
                kind, u, v, r = STEPS[a]
                if a > 0:
                    pe.wait_ge(p_ready, earlier(a))
                if kind == "swa":
                    b, g = u, v
                    pe.wait_ge(applied, APPLY_AT[f"q_a{4 * r + 3}"])
                    rows = slice(g * DA, (g + 1) * DA)
                    k0 = 0 if b else P
                    for j in range(4):
                        c0 = (j % 2) * 2 * P
                        last = mm(sc_ps[:, j // 2, c0 + k0:c0 + 2 * P],
                                  q_a[rows, 4 * r + j, b * P:(b + 1) * P],
                                  k_a[rows, (b - 1) * P + k0:(b + 1) * P], start=True, stop=True)
                elif kind == "mla":
                    h, q = u, v
                    pe.wait_ge(applied, APPLY_AT[("uk", 3)])
                    pe.wait_ge(rotated, 2)
                    pe.wait_ge(acc_free, GROUPS[("uv", 7)] + 1)
                    n = (q + 1) * P
                    out, qs = sc_ps[:, a % 2, 0:n], slice(q * P, (q + 1) * P)
                    mm(out, q_b[:, h, qs], k_b[:, h, 0:n], start=True, stop=False)
                    rows = slice(32 * h, 32 * h + 32)
                    mm(out, q_rt[rows, 0, qs], k_rt[rows, 0, 0:n], start=False, stop=False)
                    last = mm(out, q_rt[rows, 1, qs], k_rt[rows, 1, 0:n], start=False, stop=True)
                else:
                    h, q = u, v
                    last = mm(sc_ps[:, a % 2, 0:MEM], q_m[:, h, q * P:(q + 1) * P], k_m[:, h], start=True, stop=True)
                last.then_inc(scores_done, 1)

            def turn(a):
                kind = STEPS[a][0]
                pe.wait_ge(p_ready, a + 1)
                if a > 0:
                    pe.wait_ge(pt_ready, earlier(a))
                for kb in key_blocks(a):
                    if kind == "swa":
                        for j in range(4):
                            last = nc.tensor.transpose(pt_ps[:, kb, j * P:(j + 1) * P],
                                                       win_p[:, j, kb * P:(kb + 1) * P], ident[:])
                    else:
                        last = nc.tensor.transpose(pt_ps[:, a % 2, kb * P:(kb + 1) * P],
                                                   p_sb[:, a % 2, kb * P:(kb + 1) * P], ident[:])
                last.then_inc(turned, 1)

            def values(a):
                kind, u, v, r = STEPS[a]
                pe.wait_ge(pt_ready, a + 1)
                kbs = key_blocks(a)
                if kind == "swa":
                    b, g = u, v
                    if a > 0:
                        pe.wait_ge(y_done, a)
                    for kb in kbs:
                        last = mm(pv_ps[g * DA:(g + 1) * DA, 0], v_a[:, b - 1 + kb, g * DA:(g + 1) * DA],
                                  win_pt[:, kb], start=kb == kbs[0], stop=kb == kbs[-1])
                else:
                    head, q = (a - N_SWA) // NB, v
                    if q == 0:
                        pe.wait_ge(y_done, N_SWA)
                        if head >= 1:
                            pe.wait_ge(y_split, head)
                    vals = v_b if kind == "mla" else v_m
                    for kb in kbs:
                        last = mm(pv_ps[:, 0, q * P:(q + 1) * P], vals[:, kb, u * P:(u + 1) * P],
                                  pt_sb[:, a % 2, kb * P:(kb + 1) * P], start=kb == kbs[0], stop=kb == kbs[-1])
                last.then_inc(values_done, 1)

            turns_made = 0
            rep_seen = False
            for stage, i in plan:
                if stage == "slot":
                    slot(i)
                elif stage == "slot_half":
                    slot(*i)
                elif stage == "ss":
                    sum_squares(*i)
                elif stage == "v_turn":
                    pe.wait_ge(consts_made, 1)
                    pe.wait_ge(acc_free, GROUPS["v_a"] + 1)
                    for b in range(NB):
                        last = nc.tensor.transpose(pt_ps[:, 0, b * P:(b + 1) * P], tmp[:, b * P:(b + 1) * P], ident[:])
                    last.then_inc(v_turned, 1)
                elif stage == "rep":
                    pe.wait_ge(acc_free, GROUPS["k_r"] + 1)
                    pe.wait_ge(pt_ready, turns_made)
                    for j in range(2):
                        last = mm(pt_ps[:, j], rep[:, j], tmp[0:ROPE], start=True, stop=True)
                    last.then_inc(rep_done, 1)
                    rep_seen = True
                elif stage == "scores":
                    scores(i)
                elif stage == "turn":
                    if i == 0:
                        pe.wait_ge(v_copied, 1)
                    if rep_seen:
                        pe.wait_ge(rep_copied, 2)
                    turn(i)
                    turns_made += 1
                elif stage == "values":
                    values(i)

            def tile(r, s_, n, x_hi, x_lo, hidden=None):
                pe.wait_ge(lo_done, NS + s_ + 1)
                for k in range(n):
                    if hidden is not None and k >= n - 2:
                        pe.wait_ge(hid_split, hidden + k + 1)
                    last = three(acc[:, r], fw_hi[r][:, k * P:(k + 1) * P], fw_lo[r][:, k * P:(k + 1) * P],
                                 x_hi[:, k], x_lo[:, k], k == 0, k == n - 1)
                last.then_inc(slot_done, 1)

            pe.wait_ge(h_split, KC)
            with pe.Fori(0, FG) as g:
                with pe.Fori(0, FGT) as t:
                    for r in range(2):
                        tile(r, ff_slot(g, t, r), KC, f_hi, f_lo)
                with pe.Fori(0, KC // 2) as t:
                    for r in range(2):
                        tile(r, ff_slot(g, t + FGT, r), FGT, hid_hi, hid_lo, g * FGT)

        @block.scalar
        def _(act):
            A = nc.scalar

            def sq_source(name, k):
                if name in ("k_a", "k_r", "q_r"):
                    return {"k_a": k_a[:], "k_r": k_rt[:, k], "q_r": q_rt[:, k]}[name]
                if name[0] == "uq":
                    return q_b[:, name[1]]
                if name[0] == "uk":
                    return k_b[:, name[1]]
                if name == "c_q":
                    return q_b[:, k]
                if name == "c_kv":
                    return k_b[:, k]
                return q_a[:, int(name[-1])] if name.startswith("q_a") else q_m[:, int(name[-1])]

            def evacuated(name, k):
                if name in ("c_q", "c_kv"):
                    return GROUPS[f"{name}{k}"] + 1
                if name == "q_r":
                    return GROUPS[("uq", 4 + k)] + 1
                return GROUPS[name] + 1

            def split_ff(s_, pair, r, n):
                act.wait_ge(fraw_in[r], 16 * (pair + 1))
                act.wait_ge(slot_done, NS + s_ - 1)
                A.activation(fw_hi[r][:, 0:n * P], fraw[r][:, 0:n * P], ACT.Copy).then_inc(hi_done, 1)

            A.preload_act_table_set(LN_EXP_SET)
            for stage, i in plan:
                if stage == "split":
                    act.wait_ge(raw_in[PLACE[i]], 16 * USE[i])
                    if SLOT_BEFORE[i] is not None:
                        act.wait_ge(slot_done, SLOT_BEFORE[i] + 1)
                    n, r = SLOTS[i][2], PLACE[i]
                    A.activation(w_hi[r][:, 0:n], raw[r][:, 0:n], ACT.Copy).then_inc(hi_done, 1)
                elif stage == "x_pair":
                    if i == 0:
                        act.wait_ge(gain_in, 16)
                    act.wait_ge(x_in[i], 16)
                    for c in (2 * i, 2 * i + 1):
                        A.activation(xg_hi[:, c], x_sb[:, c], ACT.Copy,
                                     scale=gain[:, G_ATT + c:G_ATT + c + 1]).then_inc(xg_hi_done, 1)
                elif stage == "x_sq":
                    A.activation(x_sq[:, i], x_sb[:, i], ACT.Square).then_inc(xsq_done, 1)
                elif stage == "sines":
                    act.wait_ge(arg_made, 1)
                    A.activation(sin[:], ang[:], ACT.Sin).then_inc(sin_made, 1)
                    A.activation(cos[:], ang[:], ACT.Sin, scale=0.5).then_inc(sin_made, 1)
                    A.preload_act_table_set(LN_EXP_SET)
                elif stage == "sq":
                    name, k = i
                    n = SQ_AT[i]
                    if n <= 2:
                        act.wait_ge(ss_done, SS_END["x"])
                    elif n - 2 in SUM_OF_SQ:
                        act.wait_ge(sum_done, SUM_OF_SQ[n - 2])
                    else:
                        act.wait_ge(ss_done, SS_OF_SQ[n - 2])
                    if name == "mem":
                        act.wait_ge(mem_in, 16)
                        src = mem_raw[:, 2 * k:2 * k + 2].rearrange("p c m -> p (c m)")
                        A.activation(sq[:, (n - 1) % 2], src, ACT.Square).then_inc(sq_done, 1)
                    elif name[0] == "mem_k":
                        act.wait_ge(acc_free, GROUPS[name] + 1)
                        A.activation(sq[:, (n - 1) % 2, 0:MEM], k_m[:, name[1]], ACT.Square).then_inc(sq_done, 1)
                    else:
                        if name == "k_r":
                            act.wait_ge(rep_copied, 2)
                        else:
                            act.wait_ge(acc_free, evacuated(name, k))
                        A.activation(sq[:, (n - 1) % 2], sq_source(name, k), ACT.Square).then_inc(sq_done, 1)
                elif stage == "first_ff_splits":
                    act.wait_ge(slot_done, NS)
                    for r in range(2):
                        split_ff(r, 0, r, KC)
                elif stage == "rstd":
                    j = NORM_AT[i]
                    n_sum = {"x": D, "h": D, "mem": D, "k_a": DA, "c_q": RANK, "c_kv": RANK, "k_r": ROPE,
                             "q_r": ROPE}.get(i, DA if isinstance(i, str) and i.startswith("q_a") else P)
                    w = MEM if i == "mem" or i[0] == "mem_k" else S
                    ss_ps = ss_bank(i)
                    act.wait_ge(ss_done, SS_END[i])
                    A.activation(ss_ps[:, 0:w], ss_ps[:, 0:w], ACT.Ln, bias=eps,
                                 scale=1.0 / n_sum).then_inc(ln_done, 1)
                    act.wait_ge(ln_done, j)
                    if i not in ("x", "mem", "h") and norm_before(i, True):
                        act.wait_ge(applied, APPLY_AT[norm_before(i, True)])
                    elif i in SECOND:
                        act.wait_ge(acc_free, GROUPS["q_m3"] + 1)
                    if i == "h":
                        act.wait_ge(values_done, N_STEPS)
                    dst = {"x": rstd_x, "h": rstd_h, "mem": rstd_m}.get(i, rstd_buf(i))
                    A.activation(dst[:, 0:w], ss_ps[:, 0:w], ACT.Exp, scale=-0.5).then_inc(rstd_done, 1)
                elif stage == "v_turn":
                    act.wait_ge(v_turned, 1)
                    A.activation(v_a[:].rearrange("p b d -> p (b d)"), pt_ps[:, 0], ACT.Copy).then_inc(v_copied, 1)
                elif stage == "rep":
                    act.wait_ge(rep_done, 1)
                    for j in range(2):
                        A.activation(k_rt[:, j], pt_ps[:, j], ACT.Copy).then_inc(rep_copied, 1)
                elif stage == "mem_split":
                    act.wait_ge(mem_scaled, i + 1)
                    act.wait_ge(slot_done, SLOTS_IN - 1)
                    A.activation(mem_hi[:, 4 * i:4 * i + 4], mem_raw[:, 4 * i:4 * i + 4],
                                 ACT.Copy).then_inc(mem_hi_done, 1)
                elif stage == "c_split":
                    if i == 0:
                        act.wait_ge(applied, APPLY_AT["c_kv"])
                        act.wait_ge(slot_done, SLOTS_IN)
                    src = q_b[:, i] if i < 4 else k_b[:, i - 4]
                    A.activation(c_hi[:, i], src, ACT.Copy).then_inc(c_hi_done, 1)
                elif stage == "window_split":
                    if i == 0:
                        act.wait_ge(slot_done, SLOTS_MEM)
                        act.wait_ge(y_done, N_SWA)
                    A.activation(y_hi[:, i], q_a[:, i], ACT.Copy).then_inc(win_hi_done, 1)
                elif stage == "softmax":
                    kind, u, v, r = STEPS[i]
                    act.wait_ge(max_ready, i + 1)
                    if i == N_SWA:
                        act.wait_ge(applied, APPLY_AT[("uk", 3)])
                    nmax, sums = stat(i, 1), stat(i, 2)
                    if kind == "swa":
                        k0 = 0 if u else P
                        A.activation(stat(i, 4), stat(i, 3), ACT.Exp)
                        for j in range(4):
                            ins = A.activation(win_p[:, j, k0:], win_p[:, j, k0:], ACT.Exp, bias=nmax[:, j:j + 1],
                                               scale=DA ** -0.5, accum_out=sums[:, j:j + 1])
                        ins.then_inc(exp_done, 1)
                    elif kind == "mla":
                        w = (v + 1) * P
                        A.activation(p_sb[:, i % 2, 0:w], p_sb[:, i % 2, 0:w], ACT.Exp, bias=nmax[:, 0:1],
                                     scale=(NOPE + ROPE) ** -0.5, accum_out=sums[:, 0:1]).then_inc(exp_done, 1)
                    else:
                        if i >= N_SWA + 2:
                            act.wait_ge(turned, i - 1)
                        A.activation(p_sb[:, i % 2, 0:MEM], sc_ps[:, i % 2, 0:MEM], ACT.Exp, bias=nmax[:, 0:1],
                                     scale=P ** -0.5, accum_out=sums[:, 0:1]).then_inc(exp_done, 1)
                elif stage == "turn":
                    kind = STEPS[i][0]
                    act.wait_ge(turned, i + 1)
                    if i > 0:
                        act.wait_ge(values_done, earlier(i))
                    kbs = key_blocks(i)
                    if kind == "swa":
                        for kb in kbs:
                            ins = A.activation(win_pt[:, kb], pt_ps[:, kb], ACT.Copy)
                    else:
                        w = len(kbs) * P
                        ins = A.activation(pt_sb[:, i % 2, 0:w], pt_ps[:, i % 2, 0:w], ACT.Copy)
                    ins.then_inc(pt_ready, 1)
                elif stage == "values" and i >= N_SWA and STEPS[i][2] == NB - 1:
                    head = (i - N_SWA) // NB
                    act.wait_ge(values_done, i + 1)
                    act.wait_ge(slot_done, SLOTS_UV)
                    A.activation(y_hi[:, 8 + head], pv_ps[:, 0], ACT.Copy).then_inc(y_hi_done, 1)
                elif stage == "h_tile":
                    act.wait_ge(acc_free, GROUPS[("out_b", i)] + 1)
                    act.wait_ge(values_done, N_STEPS)
                    if i >= 2:
                        act.wait_ge(hsum_done, i - 1)
                    A.activation(hsq[:, i % 2], h_sb[:, i], ACT.Square).then_inc(hsq_done, 1)

            def gate_up(g, t, n_next):
                pair = g * PAIRS + t
                split_ff(ff_slot(g, t, 2), pair + 1, 0, n_next)
                act.wait_ge(acc_free, NGROUPS + ff_slot(g, t, 0) + 1)
                A.activation(silu_sb[:], gate_sb[:], ACT.Silu).then_inc(silu_done, 1)
                split_ff(ff_slot(g, t, 3), pair + 1, 1, n_next)
                act.wait_ge(hid_made, g * FGT + t + 1)
                A.activation(hid_hi[:, t], up_sb[:], ACT.Copy).then_inc(hid_hi_done, 1)

            def down(g, t, n_next):
                for r in range(2 if n_next else 0):
                    split_ff(ff_slot(g, t + FGT, 2 + r), g * PAIRS + FGT + t + 1, r, n_next)

            A.preload_act_table(ACT.Silu)
            ff_loops(act, gate_up, down)

        @block.vector
        def _(dve):
            V = nc.vector
            chain = [0]

            def link(ins):
                chain[0] += 1
                ins.then_inc(dve_step, 1)
                dve.wait_ge(dve_step, chain[0])

            def gained(name, k=0):
                if name == "k_a":
                    return k_a[:], G_KA
                if name in ("k_r", "q_r"):
                    return (k_rt if name == "k_r" else q_rt)[:, k], (G_KR if name == "k_r" else G_QR) + k
                if name == "c_q":
                    return q_b[:, k], G_CQ + k
                if name == "c_kv":
                    return k_b[:, k], G_CKV + k
                if name[0] == "uq":
                    return q_b[:, name[1]], G_QN
                if name[0] == "uk":
                    return k_b[:, name[1]], G_KN
                if name[0] == "mem_k":
                    return k_m[:, name[1]], G_KM
                if name.startswith("q_a"):
                    return q_a[:, int(name[-1])], G_QA
                return q_m[:, int(name[-1])], G_QM

            def apply_norm(name):
                j = NORM_AT[name]
                dve.wait_ge(rstd_done, j)
                n = {"c_q": 4, "c_kv": 4, "k_r": 2, "q_r": 2}.get(name, 1)
                w = MEM if name[0] == "mem_k" else S
                for k in range(n):
                    t, c = gained(name, k)
                    ins = V.scalar_tensor_tensor(t, t, gain[:, c:c + 1], rstd_buf(name)[:, 0:w], ALU.mult, ALU.mult)
                ins.then_inc(applied, 1)

            def evacuate(name):
                ends_slot, n = GROUP_ENDS[name]
                dve.wait_ge(slot_done if ends_slot else part_done, n)
                src = acc[:, bank_of[name]]
                if name in IN_TILES:
                    if name == "k_a":
                        dve.wait_ge(rstd_done, NORM_AT["x"])
                    if name == "k_r":
                        dve.wait_ge(v_turned, 1)
                        ins = V.tensor_tensor(tmp[0:ROPE], src[0:ROPE], rstd_x[0:ROPE], ALU.mult)
                    else:
                        dst = {"k_a": k_a[:], "v_a": tmp[:]}.get(name)
                        if dst is None:
                            buf = {"q_a": q_a, "c_q": q_b, "c_k": k_b, "q_m": q_m}[name[:3]]
                            dst = buf[:, int(name[-1])]
                        ins = V.tensor_tensor(dst, src, rstd_x[:], ALU.mult)
                elif name[0] == "mem_k":
                    ins = V.tensor_copy(k_m[:, name[1]], src[:, 0:MEM])
                elif name[0] == "mem_v":
                    ins = V.tensor_copy(v_m[:, name[1]], src)
                elif name[0] == "uq":
                    ins = V.tensor_copy(q_b[:, name[1]] if name[1] < 4 else q_rt[:, name[1] - 4], src)
                elif name[0] == "uk":
                    ins = V.tensor_copy(k_b[:, name[1]], src)
                elif name[0] == "uv":
                    s_, t = divmod(name[1], 4)
                    ins = V.tensor_copy(v_b[:, t, s_ * 2 * P:(s_ + 1) * 2 * P], src[:, 0:2 * P])
                else:
                    if name[0] == "out_a" and name[1] % 4 == 0:
                        dve.wait_ge(x_again_in[name[1] // 4], 16)
                    ins = V.tensor_tensor(h_sb[:, name[1]], src, h_sb[:, name[1]], ALU.add)
                ins.then_inc(acc_free, 1)

            def softmax(a):
                kind, u, v, r = STEPS[a]
                dve.wait_ge(scores_done, a + 1)
                mx, nmax = stat(a, 0), stat(a, 1)
                if kind == "swa":
                    b, g = u, v
                    k0 = 0 if b else P
                    if a == 0:
                        dve.wait_ge(dist_masked, NB)
                        dve.wait_ge(cos_made, 1)
                    else:
                        dve.wait_ge(turned, a)
                    for j in range(4):
                        slope = 2.0 ** (-8.0 * (g * 8 + 4 * r + j + 1) / HA)
                        c0 = (j % 2) * 2 * P
                        ins = V.scalar_tensor_tensor(win_p[:, j, k0:], dist[:, b, k0:], -slope * DA ** 0.5,
                                                     sc_ps[:, j // 2, c0 + k0:c0 + 2 * P], ALU.mult, ALU.add)
                    link(ins)
                    link(V.tensor_reduce(mx, win_p[:, :, k0:], AX.X, ALU.max))
                    heads = slice(g * 8 + 4 * r, g * 8 + 4 * r + 4)
                    link(V.scalar_tensor_tensor(nmax, mx, -DA ** -0.5, nsink[:, heads], ALU.mult, ALU.min))
                    V.tensor_tensor(stat(a, 3), sink[:, heads], nmax, ALU.add).then_inc(max_ready, 1)
                elif kind == "mla":
                    w = (v + 1) * P
                    if a >= N_SWA + 2:
                        dve.wait_ge(turned, a - 1)
                    else:
                        dve.wait_ge(applied, APPLY_AT[("uk", 3)])
                    link(V.tensor_tensor(p_sb[:, a % 2, 0:w], sc_ps[:, a % 2, 0:w],
                                         causal[:, S - w:], ALU.add))
                    link(V.tensor_reduce(mx[:, 0:1], p_sb[:, a % 2, 0:w], AX.X, ALU.max))
                    V.tensor_scalar(nmax[:, 0:1], mx[:, 0:1], -(NOPE + ROPE) ** -0.5, None,
                                    ALU.mult).then_inc(max_ready, 1)
                else:
                    link(V.tensor_reduce(mx[:, 0:1], sc_ps[:, a % 2, 0:MEM], AX.X, ALU.max))
                    V.tensor_scalar(nmax[:, 0:1], mx[:, 0:1], -P ** -0.5, None, ALU.mult).then_inc(max_ready, 1)

            def p_norm(a):
                kind, u, v, r = STEPS[a]
                dve.wait_ge(exp_done, a + 1)
                sums, rec = stat(a, 2), stat(a, 6)
                if kind == "swa":
                    k0 = 0 if u else P
                    den = stat(a, 5)
                    link(V.tensor_tensor(den, sums, stat(a, 4), ALU.add))
                    link(V.reciprocal(rec, den))
                    for j in range(4):
                        ins = V.tensor_scalar(win_p[:, j, k0:], win_p[:, j, k0:], rec[:, j:j + 1], None, ALU.mult)
                else:
                    w = len(key_blocks(a)) * P
                    link(V.reciprocal(rec[:, 0:1], sums[:, 0:1]))
                    ins = V.tensor_scalar(p_sb[:, a % 2, 0:w], p_sb[:, a % 2, 0:w], rec[:, 0:1], None, ALU.mult)
                ins.then_inc(p_ready, 1)

            def split_ff(s_, r, n):
                dve.wait_ge(hi_done, NS + s_ + 1)
                V.tensor_tensor(fw_lo[r][:, 0:n * P], fraw[r][:, 0:n * P], fw_hi[r][:, 0:n * P].bitcast(F32),
                                ALU.subtract).then_inc(lo_done, 1)

            for stage, i in plan:
                if stage == "first_ff_splits":
                    for r in range(2):
                        split_ff(r, r, KC)
                elif stage == "split":
                    n = SLOTS[i][2]
                    dve.wait_ge(hi_done, i + 1)
                    r = PLACE[i]
                    V.tensor_tensor(w_lo[r][:, 0:n], raw[r][:, 0:n], w_hi[r][:, 0:n].bitcast(F32),
                                    ALU.subtract).then_inc(lo_done, 1)
                elif stage == "x_pair":
                    for c in (2 * i, 2 * i + 1):
                        dve.wait_ge(xg_hi_done, c + 1)
                        V.scalar_tensor_tensor(xg_lo[:, c], x_sb[:, c], gain[:, G_ATT + c:G_ATT + c + 1],
                                               xg_hi[:, c].bitcast(F32), ALU.mult, ALU.subtract).then_inc(xg_done, 1)
                elif stage == "x_sq" and i % 2:
                    dve.wait_ge(xsq_done, i + 1)
                    if i == 1:
                        V.tensor_copy(xsum_odd[:], x_sq[:, i]).then_inc(xodd_done, 1)
                    else:
                        dve.wait_ge(xodd_done, i // 2)
                        V.tensor_tensor(xsum_odd[:], xsum_odd[:], x_sq[:, i], ALU.add).then_inc(xodd_done, 1)
                elif stage == "setup":
                    dve.wait_ge(small_in, 64)
                    dve.wait_ge(xsq_done, KC)
                    V.tensor_copy(pos_f[:], pos_i[:])
                    V.tensor_scalar(nsink[:], sink[:], -1.0, None, ALU.mult)
                    link(V.tensor_copy(pos_q[:], pos_qi[:]))
                    for b in range(NB):
                        k0 = 0 if b else P
                        link(V.tensor_scalar(dist[:, b, k0:], pos_f[:, (b - 1) * P + k0:(b + 1) * P],
                                             pos_q[:, b:b + 1], None, ALU.subtract))
                        V.scalar_tensor_tensor(dist[:, b, k0:], dist[:, b, k0:], -1.0, dist[:, b, k0:], ALU.mult,
                                               ALU.max).then_inc(dist_made, 1)
                elif stage == "angles":
                    link(V.tensor_scalar(ang[:], pos_f[:], invf, None, ALU.mult))
                    link(V.tensor_scalar(turns[:], ang[:], 1.0 / TWO_PI, MAGIC, ALU.mult, ALU.add))
                    link(V.tensor_scalar(turns[:], turns[:], -MAGIC, None, ALU.add))
                    for part in (C1, C2, C3):
                        link(V.scalar_tensor_tensor(ang[:], turns[:], -part, ang[:], ALU.mult, ALU.add))
                    V.tensor_scalar(ang[:], ang[:], 3.1415925, -3.1415925, ALU.min, ALU.max).then_inc(arg_made, 1)
                elif stage == "sines":
                    dve.wait_ge(sin_made, 2)
                    link(V.tensor_tensor(cos[:], cos[:], cos[:], ALU.mult))
                    V.tensor_scalar(cos[:], cos[:], -2.0, 1.0, ALU.mult, ALU.add).then_inc(cos_made, 1)
                elif stage == "apply":
                    apply_norm(i)
                elif stage == "evac":
                    evacuate(i)
                elif stage == "mem_scale":
                    dve.wait_ge(rstd_done, NORM_AT["mem"])
                    for c in range(4 * i, 4 * i + 4):
                        ins = V.scalar_tensor_tensor(mem_raw[:, c], mem_raw[:, c], gain[:, G_MEM + c:G_MEM + c + 1],
                                                     rstd_m[:], ALU.mult, ALU.mult)
                    ins.then_inc(mem_scaled, 1)
                elif stage == "mem_split":
                    dve.wait_ge(mem_hi_done, i + 1)
                    V.tensor_tensor(mem_lo[:, 4 * i:4 * i + 4], mem_raw[:, 4 * i:4 * i + 4],
                                    mem_hi[:, 4 * i:4 * i + 4].bitcast(F32), ALU.subtract).then_inc(mem_split, 1)
                elif stage == "c_split":
                    dve.wait_ge(c_hi_done, i + 1)
                    src = q_b[:, i] if i < 4 else k_b[:, i - 4]
                    V.tensor_tensor(c_lo[:, i], src, c_hi[:, i].bitcast(F32), ALU.subtract).then_inc(c_split, 1)
                elif stage == "window_split":
                    dve.wait_ge(win_hi_done, i + 1)
                    V.tensor_tensor(y_lo[:, i], q_a[:, i], y_hi[:, i].bitcast(F32), ALU.subtract).then_inc(win_split, 1)
                elif stage == "softmax":
                    softmax(i)
                elif stage == "p_norm":
                    p_norm(i)
                elif stage == "values":
                    kind, u, v, r = STEPS[i]
                    if kind == "swa":
                        dve.wait_ge(values_done, i + 1)
                        rows = slice(v * DA, (v + 1) * DA)
                        V.tensor_copy(q_a[rows, 4 * r:4 * r + 4, u * P:(u + 1) * P],
                                      pv_ps[rows, 0].rearrange("p (h q) -> p h q", h=4)).then_inc(y_done, 1)
                    elif v == NB - 1:
                        head = (i - N_SWA) // NB
                        dve.wait_ge(y_hi_done, head + 1)
                        V.tensor_tensor(y_lo[:, 8 + head], pv_ps[:, 0], y_hi[:, 8 + head].bitcast(F32),
                                        ALU.subtract).then_inc(y_split, 1)
                elif stage == "h_tile":
                    if i == 0:
                        dve.wait_ge(values_done, N_STEPS)
                    dve.wait_ge(acc_free, GROUPS[("out_b", i)] + 1)
                    g = gain[:, G_FFN + i:G_FFN + i + 1]
                    link(V.tensor_scalar(f_hi[:, i], h_sb[:, i], g, None, ALU.mult))
                    V.scalar_tensor_tensor(f_lo[:, i], h_sb[:, i], g, f_hi[:, i].bitcast(F32), ALU.mult,
                                           ALU.subtract).then_inc(h_split, 1)

            def gate_up(g, t, n_next):
                n = g * FGT + t
                dve.wait_ge(slot_done, NS + ff_slot(g, t, 0) + 1)
                V.tensor_tensor(gate_sb[:], acc[:, 0], rstd_h[:], ALU.mult).then_inc(acc_free, 1)
                split_ff(ff_slot(g, t, 2), 0, n_next)
                dve.wait_ge(slot_done, NS + ff_slot(g, t, 1) + 1)
                V.tensor_tensor(up_sb[:], acc[:, 1], rstd_h[:], ALU.mult).then_inc(acc_free, 1)
                dve.wait_ge(acc_free, NGROUPS + ff_slot(g, t, 1) + 1)
                dve.wait_ge(silu_done, n + 1)
                V.tensor_tensor(up_sb[:], up_sb[:], silu_sb[:], ALU.mult).then_inc(hid_made, 1)
                dve.wait_ge(hid_hi_done, n + 1)
                V.tensor_tensor(hid_lo[:, t], up_sb[:], hid_hi[:, t].bitcast(F32),
                                ALU.subtract).then_inc(hid_split, 1)
                split_ff(ff_slot(g, t, 3), 1, n_next)

            def down(g, t, n_next):
                for r in range(2):
                    dve.wait_ge(slot_done, NS + ff_slot(g, t + FGT, r) + 1)
                    V.tensor_tensor(h_sb[:, t * 2 + r], acc[:, r], h_sb[:, t * 2 + r], ALU.add).then_inc(acc_free, 1)
                    if n_next:
                        split_ff(ff_slot(g, t + FGT, 2 + r), r, n_next)

            dve.wait_ge(rstd_done, NORM_AT["h"])
            ff_loops(dve, gate_up, down)

        @block.gpsimd
        def _(pool):
            G = nc.gpsimd
            chain = [0]

            def link(ins):
                chain[0] += 1
                ins.then_inc(pool_step, 1)
                pool.wait_ge(pool_step, chain[0])

            G.memset(ones[:], 1.0)
            G.memset(blk64[:], 1.0)
            G.memset(blk32[:], 1.0)
            G.memset(ident[:], 0.0)
            G.memset(rep[:], 0.0)
            G.memset(eps, EPS)
            link(G.memset(causal[:], 0.0))
            link(G.affine_select(out=ident[:], in_=ident[:], compare_op=ALU.not_equal, fill=1.0, base=0,
                                 pattern=[[-1, P]], channel_multiplier=1))
            for blk, n in ((blk64, DA), (blk32, 32)):
                v = blk[:].rearrange("p (b d) -> p b d", d=n)
                link(G.affine_select(out=v, in_=v, compare_op=ALU.is_ge, fill=0.0, base=0,
                                     pattern=[[-n, P // n], [0, n]], channel_multiplier=1))
                link(G.affine_select(out=v, in_=v, compare_op=ALU.is_ge, fill=0.0, base=n - 1,
                                     pattern=[[n, P // n], [0, n]], channel_multiplier=-1))
            for j in range(2):
                v = rep[:, j].rearrange("p (h d) -> p h d", d=32)
                link(G.affine_select(out=v, in_=v, compare_op=ALU.not_equal, fill=1.0, base=-32 * j,
                                     pattern=[[0, 4], [-1, 32]], channel_multiplier=1))
            G.affine_select(out=causal[:, S - P:], in_=causal[:, S - P:], compare_op=ALU.is_ge, fill=-FILL, base=0,
                            pattern=[[-1, P]], channel_multiplier=1).then_inc(consts_made, 1)
            for c in range(0, KC, 2):
                pool.wait_ge(xsq_done, c + 1)
                if c == 0:
                    G.tensor_copy(xsum[:], x_sq[:, 0]).then_inc(xsum_done, 1)
                else:
                    pool.wait_ge(xsum_done, c // 2)
                    G.tensor_tensor(xsum[:], xsum[:], x_sq[:, c], ALU.add).then_inc(xsum_done, 1)
            for b in range(NB):
                pool.wait_ge(dist_made, b + 1)
                k0 = 0 if b else P
                if b:
                    link(G.affine_select(out=dist[:, b], in_=dist[:, b], compare_op=ALU.is_ge, fill=FILL, base=-1,
                                         pattern=[[1, 2 * P]], channel_multiplier=-1))
                G.affine_select(out=dist[:, b, k0:], in_=dist[:, b, k0:], compare_op=ALU.is_ge, fill=FILL,
                                base=P - k0, pattern=[[-1, 2 * P - k0]], channel_multiplier=1).then_inc(dist_masked, 1)
            for stage, i in plan:
                if stage == "rotate":
                    pool.wait_ge(applied, APPLY_AT[i])
                    pool.wait_ge(cos_made, 1)
                    if i == "q_r":
                        pool.wait_ge(rotated, 1)
                    x1, x2 = (k_rt if i == "k_r" else q_rt)[:, 0], (k_rt if i == "k_r" else q_rt)[:, 1]
                    G.tensor_tensor(tmp[:], x1, cos[:], ALU.mult)
                    G.tensor_tensor(pos_f[:], x2, sin[:], ALU.mult)
                    G.tensor_tensor(xsum[:], x1, sin[:], ALU.mult)
                    link(G.tensor_tensor(x2, x2, cos[:], ALU.mult))
                    link(G.tensor_tensor(x1, tmp[:], pos_f[:], ALU.subtract))
                    G.tensor_tensor(x2, x2, xsum[:], ALU.add).then_inc(rotated, 1)
                if stage != "sum":
                    continue
                name, k = i
                pool.wait_ge(sq_done, SQ_AT[i])
                src = sq[:, (SQ_AT[i] - 1) % 2]
                if k == 0:
                    pool.wait_ge(ss_done, SS_END[{"mem": "x", "c_q": "mem", "c_kv": "c_q"}[name]])
                    G.tensor_copy(xsum[:], src).then_inc(sum_done, 1)
                else:
                    pool.wait_ge(sum_done, SUM_AT[i] - 1)
                    G.tensor_tensor(xsum[:], xsum[:], src, ALU.add).then_inc(sum_done, 1)
            for m in range(KC):
                pool.wait_ge(hsq_done, m + 1)
                if m == 0:
                    G.tensor_copy(ssum[:], hsq[:, 0]).then_inc(hsum_done, 1)
                else:
                    pool.wait_ge(hsum_done, m)
                    G.tensor_tensor(ssum[:], ssum[:], hsq[:, m % 2], ALU.add).then_inc(hsum_done, 1)
            for m in range(KC // 2):
                last_t = ff_slot(FG - 1, FGT + m, 1)
                pool.wait_ge(acc_free, NGROUPS + last_t + 1)
                G.dma_start(outT[:, 2 * m:2 * m + 2], h_sb[:, 2 * m:2 * m + 2]).then_inc(out_sent, 16)
            pool.wait_ge(out_sent, 16 * (KC // 2))


def _tiles(w, n):
    k, m = w.shape
    return np.ascontiguousarray(w.reshape(k // P, P, m // n, n).transpose(2, 1, 0, 3)).reshape(m // n, P, k // P * n)


def _halves(w, n):
    k, m = w.shape
    return np.ascontiguousarray(
        w.reshape(2, k // P // 2, P, m // n, n).transpose(3, 0, 2, 1, 4)).reshape(m // n, 2, P, k // P // 2 * n)


def lay_out(i):
    col = lambda g: g.reshape(-1, P).T
    x, mem, pos = i["x"][0], i["mem"][0], i["positions"][0]
    w = i["w_in"][0]
    cuts = np.cumsum([0, HA * DA, GA * DA, GA * DA, RANK, RANK, ROPE, HM * P])
    wq, wk, wv, wcq, wckv, wkr, wqm = (w[:, a:b] for a, b in zip(cuts[:-1], cuts[1:]))
    wq = wq.reshape(D, GA, 8, DA).transpose(0, 2, 1, 3).reshape(D, HA * DA)
    big = np.concatenate([wk, wv, wq, wcq, wckv, wqm], axis=1)
    mkv = i["w_mem_kv"][0]
    uq = i["w_uq"][0].reshape(RANK, HB, NOPE + ROPE)
    halves = uq[:, :, NOPE:].reshape(RANK, HB, 2, 32).transpose(0, 2, 1, 3).reshape(RANK, HB * ROPE)
    uq = np.concatenate([uq[:, :, :NOPE].reshape(RANK, HB * NOPE), halves], axis=1)
    ukv = i["w_ukv"][0].reshape(RANK, HB, 2, P)
    wo = i["w_out"][0]
    wo_a = wo[:HA * DA].reshape(GA, 8, DA, D).transpose(1, 0, 2, 3).reshape(HA * DA, D)
    gu = np.stack([_tiles(i["w_gate"][0], P), _tiles(i["w_up"][0], P)], axis=1).reshape(2 * FT, P, KC * P)
    dn = i["w_down"][0].reshape(FG, FGT, P, KC, P).transpose(0, 3, 2, 1, 4)
    four = lambda g: np.tile(g, 4)[:, None]
    two = lambda g: np.tile(g, 2)[:, None]
    kr, qr = i["mla_kr_norm_g"][0], i["mla_qr_norm_g"][0]
    gains = np.concatenate([
        col(i["attn_norm_g"][0]), col(i["ffn_norm_g"][0]), col(i["mem_norm_g"][0]),
        two(i["swa_q_norm_g"][0]), two(i["swa_k_norm_g"][0]), col(i["mla_cq_norm_g"][0]),
        col(i["mla_ckv_norm_g"][0]), i["mla_qn_norm_g"][0][:, None], i["mla_kn_norm_g"][0][:, None],
        four(qr[:32]), four(qr[32:]), four(kr[:32]), four(kr[32:]),
        i["mem_q_norm_g"][0][:, None], i["mem_k_norm_g"][0][:, None]], axis=1)
    freq = (10000.0 ** (-np.arange(0, ROPE, 2, dtype=np.float32) / np.float32(ROPE))).astype(np.float32)
    chunks = lambda a: a.T.reshape(KC, P, -1).transpose(1, 0, 2)
    pairs = lambda t: t.reshape(t.shape[0] // 2, 2, P, -1).transpose(0, 2, 1, 3).reshape(t.shape[0] // 2, P, -1)
    vs = lambda w_, c, n: w_.reshape(-1, c, P, n).transpose(0, 2, 1, 3).reshape(-1, P, c * n)
    uv = ukv[:, :, 1].reshape(RANK, 2, 2 * P).transpose(1, 0, 2)
    return {
        "xT": chunks(x), "memT": chunks(mem), "pos_rows": np.broadcast_to(pos[None], (P, S)),
        "pos_cols": pos.reshape(NB, P).T, "gains": gains,
        "sink_rows": np.broadcast_to(i["swa_sinks"][0][None], (P, HA)), "inv_freq": four(freq),
        "w_in": _halves(big, P), "w_kr": _halves(wkr, ROPE)[0],
        "w_memk": _halves(mkv[:, :HM * P], P), "w_memv": vs(mkv[:, HM * P:], 2, HM * P),
        "w_uq": pairs(_tiles(uq, P)), "w_uk": pairs(_tiles(ukv[:, :, 0].reshape(RANK, HB * P), P)),
        "w_uv": np.stack([vs(uv[k], 4, 2 * P)[0] for k in range(2)]),
        "w_outa": _tiles(wo_a, P), "w_outb": _tiles(wo[HA * DA:], P),
        "w_gu": gu, "w_dn": dn.reshape(FG * KC, P, FGT * P),
    }


def kernel(**inputs):
    import concourse.bacc as bacc
    from concourse.bass_utils import run_bass_kernel_spmd

    nc = bacc.Bacc("TRN2", target_bir_lowering=False, num_devices=1)
    arrays = {k: np.ascontiguousarray(v) for k, v in lay_out({k: np.asarray(v) for k, v in inputs.items()}).items()}
    aps = {k: nc.dram_tensor(k, v.shape, mybir.dt.from_np(v.dtype), kind="ExternalInput").ap()
           for k, v in arrays.items()}
    outT = nc.dram_tensor("outT", (P, KC, S), F32, kind="ExternalOutput").ap()
    build_layer(nc, **aps, outT=outT)
    got = run_bass_kernel_spmd(nc, [arrays], core_ids=[0]).results[0]["outT"]
    return np.ascontiguousarray(got.transpose(2, 1, 0).reshape(1, S, D))
```

```python
from contextlib import ExitStack

import numpy as np

import concourse.bass as bass
from concourse import mybir

ALU = mybir.AluOpType
ACT = mybir.ActivationFunctionType
AX = mybir.AxisListType
F32 = mybir.dt.float32
F32R = mybir.dt.float32r
I32 = mybir.dt.int32

P = 128
D = 2048
S = 512
MEM = 256
EPS = 1e-6
HA, GA, DA = 16, 2, 64
HB, NOPE, ROPE, RANK = 4, 128, 64, 512
HM = 4
DFF = ((8 * D + 3 * 256 - 1) // (3 * 256)) * 256
KC = D // P
NB = S // P
FT = DFF // P
FG = 4
FGT = FT // FG
SUB = 8
FILL = 1e30

IN_TILES = (["k_a", "v_a"] + [f"q_a{i}" for i in range(8)] + [f"c_q{i}" for i in range(4)]
            + [f"c_kv{i}" for i in range(4)] + ["k_r"] + [f"q_m{i}" for i in range(4)])
N_IN = len(IN_TILES)

SLOTS = []
for _i, _half in [(0, 0), (1, 0), (0, 1), (1, 1)] + [(t, half) for t in range(2, N_IN) for half in range(2)]:
    SLOTS.append(("in", (_i, _half), SUB * (ROPE if IN_TILES[_i] == "k_r" else P)))
for _i in range(HM):
    for _half in range(2):
        SLOTS.append(("mem_k", (_i, _half), SUB * P))
for _i in range(KC // 2):
    SLOTS.append(("mem_v", _i, SUB * P))
for _i in range(3):
    SLOTS.append(("uq", _i, SUB * P))
for _i in range(2):
    SLOTS.append(("uk", _i, SUB * P))
for _i in range(2):
    SLOTS.append(("uv", _i, SUB * P))
for _i in range(KC):
    SLOTS.append(("out_a", _i, SUB * P))
for _i in range(KC):
    SLOTS.append(("out_b", _i, SUB * P))
NS = len(SLOTS)

SLOTS_IN = 2 * N_IN
SLOTS_MEM = SLOTS_IN + 2 * HM + KC // 2
SLOTS_UV = SLOTS_MEM + 7


def make_ring():
    place, before, last = [], [], {}
    for i in range(NS):
        n = 3 if SLOTS_IN + 4 <= i < SLOTS_UV else 2
        free = [r for r in range(n) if r not in place[len(place) - n + 1:]] if i else [0]
        place.append(min(free, key=lambda r: last.get(r, -1)))
        before.append(last.get(place[-1]))
        last[place[-1]] = i
    return place, before


PLACE, SLOT_BEFORE = make_ring()
USE = [sum(q == PLACE[i] for q in PLACE[:i + 1]) for i in range(NS)]
THIRD = PLACE.index(2)

GROUPS = {}


def _group(name):
    GROUPS[name] = len(GROUPS)


for _n in IN_TILES:
    _group(_n)
for _i in range(HM):
    _group(("mem_k", _i))
for _i in range(MEM // P):
    _group(("mem_v", _i))
for _i in range(6):
    _group(("uq", _i))
for _i in range(4):
    _group(("uk", _i))
for _i in range(8):
    _group(("uv", _i))
for _i in range(KC):
    _group(("out_a", _i))
for _i in range(KC):
    _group(("out_b", _i))
NGROUPS = len(GROUPS)

STEPS = [("swa", b, g, r) for r in range(2) for b in range(NB) for g in range(GA)]
STEPS += [("mla", h, q, 0) for h in range(HB) for q in range(NB)]
STEPS += [("mem", h, q, 0) for h in range(HM) for q in range(NB)]
N_SWA = 16
N_STEPS = len(STEPS)

G_ATT, G_FFN, G_MEM, G_QA, G_KA, G_CQ, G_CKV = 0, 16, 32, 48, 49, 50, 54
G_QN, G_KN, G_QR, G_KR, G_QM, G_KM, G_ALL = 58, 59, 60, 61, 62, 63, 64

TWO_PI = 2 * np.pi
C1 = 6.28125
C2 = float(np.float32(np.round((TWO_PI - C1) * 2 ** 20) / 2 ** 20))
C3 = float(np.float32(TWO_PI - C1 - C2))
MAGIC = 1.5 * 2 ** 23
LN_EXP_SET = "natural_log_exp_and_others"


def make_plan():
    plan = []
    late = []
    state = {"slot": 0, "split": 2}

    def next_splits(i):
        while state["split"] < NS:
            n = state["split"]
            if (SLOTS_IN + 1 if n == THIRD else SLOT_BEFORE[n]) > i:
                break
            plan.append(("split", n))
            state["split"] += 1

    def run_slot(before_split=(), after_split=()):
        i = state["slot"]
        state["slot"] += 1
        plan.append(("slot", i))
        plan.extend(before_split)
        next_splits(i)
        while late:
            plan.extend(late.pop(0))
        plan.extend(after_split)

    def norm(name, n=1):
        return [("ss", (name, k, n)) for k in range(n)] + [("rstd", name), ("apply", name)]

    pair = lambda *js: [("x_pair", j) for j in js]
    squares = lambda lo, hi: [("x_sq", c) for c in range(lo, hi)]
    plan.extend([("split", 0)] + pair(0, 1, 2) + [("split", 1)] + pair(3) + squares(0, 1))
    run_slot(pair(4) + squares(1, 3) + pair(5) + squares(3, 4))
    run_slot(pair(6, 7) + squares(4, 8), squares(8, 12))
    run_slot(squares(12, KC))
    run_slot()
    plan.extend([("ss", ("x", 0, 1)), ("rstd", "x"), ("evac", "k_a"), ("sq", ("k_a", 0)), ("evac", "v_a")])
    late.append(norm("k_a") + [("v_turn", 0), ("setup", 0)])
    step = None
    squared = iter(range(KC // 2))

    def mem_square():
        k = next(squared)
        plan.extend([("sq", ("mem", k)), ("sum", ("mem", k))])

    for name in IN_TILES[2:]:
        begun = step is not None
        run_slot([("p_norm", step)] if begun else [], [("values", step - 1)] if step else [])
        if name in ("q_a1", "q_a2", "q_a3", "q_a4"):
            mem_square()
        if name in ("q_a6", "q_a7"):
            plan.append(("mem_scale", 2 * (name == "q_a7")))
        last = name == IN_TILES[-1]
        if name in ("q_a1", "q_a2", "q_a3", "q_a4"):
            mem_square()
        if name in ("q_a6", "q_a7"):
            plan.append(("mem_scale", 1 + 2 * (name == "q_a7")))
        if last:
            plan.extend([("mem_split", j) for j in range(4)])
        run_slot([], {"q_a5": [("ss", ("mem", 0, 1)), ("rstd", "mem")], "q_m0": norm("k_r")}.get(name, []))
        plan.append(("evac", name))
        if name[:2] == "c_":
            base, k = name[:-1], int(name[-1])
            plan.extend([("sq", (base, k)), ("sum", (base, k))])
            if k == 3:
                late.append([("ss", (base, 0, 1)), ("rstd", base), ("apply", base)])
        elif name == "k_r":
            late.append([("rep", 0), ("sq", (name, 0))])
        else:
            plan.append(("sq", (name, 0)))
            late.append(norm(name))
        if name == "q_a4":
            step = 0
            plan.extend([("scores", 0), ("softmax", 0)])
        elif step is not None:
            plan.append(("turn", step))
            step += 1
            if step < N_SWA:
                plan.extend([("scores", step), ("softmax", step)])
        if name == "q_a0":
            plan.extend([("mem_load", 0), ("angles", 0)])
        if name == "q_a1":
            plan.append(("sines", 0))
    assert step == N_SWA
    for i in range(HM):
        run_slot([], [("c_split", 2 * i)] + ([("values", N_SWA - 1)] if i == 0 else []))
        run_slot([("evac", ("mem_k", i)), ("sq", (("mem_k", i), 0))],
                 [("c_split", 2 * i + 1)] + ([("swap", 0)] if i == 1 else []))
        late.append(norm(("mem_k", i)))
    for i in range(KC // 2):
        run_slot([("evac", ("mem_v", 0)), ("evac", ("mem_v", 1))] if i == KC // 2 - 1 else [])

    def two_heads(kind, i, after):
        this = []
        for m in (2 * i, 2 * i + 1):
            this.extend([("evac", (kind, m)), ("sq", ((kind, m), 0))])
        run_slot(this, after)
        late.extend(norm((kind, m)) for m in (2 * i, 2 * i + 1))

    windows = [("window_split", k) for k in range(SUB)]
    two_heads("uq", 0, windows[0:2])
    plan.append(("x_again", 0))
    two_heads("uq", 1, windows[2:4])
    plan.append(("x_again", 1))
    two_heads("uq", 2, windows[4:6])
    two_heads("uk", 0, windows[6:8])
    two_heads("uk", 1, [])
    delayed = [("apply", ("uk", m)) for m in range(2)]
    for a in delayed:
        plan.remove(a)
    for i in range(2):
        evacs = [("evac", ("uv", m)) for m in range(4 * i, 4 * i + 4)]
        run_slot(evacs[:2] + (delayed if i == 0 else []) + evacs[2:], [("swap", 1), ("swap", 2)] if i == 0 else [])

    def later_piece(n):
        if N_SWA <= n - 1 < N_STEPS:
            plan.append(("p_norm", n - 1))
        if N_SWA <= n - 3 < N_STEPS:
            plan.append(("values", n - 3))
        if N_SWA <= n - 2 < N_STEPS:
            plan.append(("turn", n - 2))
        if n < N_STEPS:
            plan.extend([("scores", n), ("softmax", n)])

    n = N_SWA
    for m in range(KC):
        i = state["slot"]
        state["slot"] += 1
        plan.append(("slot_part", (i, 0, SUB // 2)))
        later_piece(n)
        plan.append(("slot_part", (i, SUB // 2, SUB)))
        later_piece(n + 1)
        n += 2
        next_splits(i)
        plan.append(("evac", ("out_a", m)))
        if m in (2, 4):
            plan.append(("x_again", 1 + m // 2))
    i = state["slot"]
    state["slot"] += 2
    for k, part in enumerate([(i, 0, 3), (i, 3, 5), (i, 5, 7)]):
        plan.append(("slot_part", part))
        later_piece(n + k)
    plan.extend([("slot_part", (i + 1, 0, 4)), ("slot_part", (i, 7, SUB))])
    next_splits(i)
    plan.extend([("evac", ("out_b", 0)), ("h_tile", 0), ("slot_part", (i + 1, 4, SUB))])
    next_splits(i + 1)
    plan.extend([("evac", ("out_b", 1)), ("h_tile", 1)])
    for m in range(2, KC):
        run_slot()
        if m == KC - 4:
            plan.append(("first_ff_load", 0))
        if m == KC - 2:
            plan.append(("first_ff_split", 0))
        plan.extend([("evac", ("out_b", m)), ("h_tile", m)])
    plan.extend([("first_ff_split", 1), ("first_ff_tile", 0), ("ss", ("h", 0, 1)), ("rstd", "h")])
    assert state["slot"] == NS
    return plan


PLAN = make_plan()


def count(stage):
    return {i: n + 1 for n, i in enumerate(i for s, i in PLAN if s == stage)}


SQ_AT = count("sq")
SUM_AT = count("sum")
SS_AT = count("ss")
NORM_AT = count("rstd")
APPLY_AT = count("apply")
SECOND = {n for n in NORM_AT if n[0] in ("mem_k", "uq", "uk") and n[1] % 2}


def norm_before(name, own):
    same = [n for n in NORM_AT if (n in SECOND) == (name in SECOND) and not (own and n in ("x", "mem", "h"))]
    same = [n for n in same if NORM_AT[n] < NORM_AT[name]]
    return same[-1] if same else None


SS_END = {}
for (_n, _k, _m), _c in SS_AT.items():
    SS_END[_n] = _c
SS_OF_SQ = {SQ_AT[(_n, _k)]: _c for (_n, _k, _m), _c in SS_AT.items()
            if (_n, _k) in SQ_AT and (_n, _k) not in SUM_AT}
SUM_OF_SQ = {SQ_AT[_i]: _c for _i, _c in SUM_AT.items()}


SUM_END = {_n: _c for (_n, _k), _c in SUM_AT.items()}


def group_ends():
    ends, parts = {}, 0
    for i, (kind, at_, _) in enumerate(SLOTS):
        if kind == "in" and at_[1]:
            ends[IN_TILES[at_[0]]] = (True, i + 1)
        elif kind == "mem_k" and at_[1]:
            ends[("mem_k", at_[0])] = (True, i + 1)
        elif kind == "mem_v" and at_ == KC // 2 - 1:
            parts += 1
            ends[("mem_v", 0)] = (False, parts)
            ends[("mem_v", 1)] = (True, i + 1)
        elif kind in ("uq", "uk", "uv"):
            n = 4 if kind == "uv" else 2
            for j in range(n):
                last = j == n - 1
                parts += not last
                ends[(kind, n * at_ + j)] = (last, i + 1 if last else parts)
        elif kind in ("out_a", "out_b"):
            ends[(kind, at_)] = (True, i + 1)
    return ends


GROUP_ENDS = group_ends()


def build_layer(nc, xT, memT, pos_rows, pos_cols, gains, sink_rows, inv_freq, w_in, w_kr, w_memk, w_memv,
                w_uq, w_uk, w_uv, w_outa, w_outb, w_gu, w_dn, outT):
    plan = PLAN

    with ExitStack() as ctx:
        def sem(name):
            return ctx.enter_context(nc.semaphore(name))

        base = (nc.sbuf_base + 63) // 64 * 64
        KB = 1024
        H0 = base
        B0 = H0 + 32 * KB
        A0 = B0 + 64 * KB
        S0 = A0 + 64 * KB
        C0 = S0 + 24 * KB
        top = [0]

        def at(name, shape, off, dt=F32):
            return nc.alloc_sbuf_tensor_at(name, shape, dt, offset=off)

        def bump(name, shape, dt=F32):
            n = 4
            for s_ in shape[1:]:
                n *= s_
            t = at(name, shape, C0 + top[0], dt)
            top[0] += (n + 31) // 32 * 32
            return t

        x_sb = at("x_sb", [P, KC, S], H0)
        mem_raw = at("mem_raw", [P, KC, MEM], H0)
        win_p = at("win_p", [P, 4, 2 * P], H0 + 16 * KB)
        win_pt = at("win_pt", [P, 2, 4 * P], H0 + 20 * KB)
        dist = at("dist", [P, NB, 2 * P], H0 + 24 * KB)
        cos = at("cos", [P, S], H0 + 28 * KB)
        sin = at("sin", [P, S], H0 + 30 * KB)
        ang = at("ang", [P, S], H0 + 16 * KB)
        turns = at("turns", [P, S], H0 + 18 * KB)
        h_sb = at("h_sb", [P, KC, S], H0)

        q_a = at("q_a", [P, 8, S], B0)
        x_sq = at("x_sq", [P, KC, S], B0)
        q_m = at("q_m", [P, HM, S], B0 + 16 * KB)
        q_b = at("q_b", [P, 4, S], B0 + 24 * KB)
        k_b = at("k_b", [P, 4, S], B0 + 32 * KB)
        k_rt = at("k_rt", [P, S], B0 + 40 * KB)
        q_rt = at("q_rt", [P, 2, S], B0 + 44 * KB)
        v_b = at("v_b", [P, NB, HB * P], B0 + 48 * KB)
        k_m = at("k_m", [P, HM, MEM], B0 + 56 * KB)
        v_m = at("v_m", [P, 2, HM * P], B0 + 60 * KB)
        f_hi = at("f_hi", [P, KC, S], B0, F32R)
        f_lo = at("f_lo", [P, KC, S], B0 + 32 * KB, F32R)

        xg_hi = at("xg_hi", [P, KC, S], A0, F32R)
        xg_lo = at("xg_lo", [P, KC, S], A0 + 32 * KB, F32R)
        mem_hi = at("mem_hi", [P, KC, MEM], A0, F32R)
        mem_lo = at("mem_lo", [P, KC, MEM], A0 + 32 * KB, F32R)
        c_hi = at("c_hi", [P, 8, S], A0 + 16 * KB, F32R)
        c_lo = at("c_lo", [P, 8, S], A0 + 48 * KB, F32R)
        y_hi = at("y_hi", [P, KC, S], A0, F32R)
        y_lo = at("y_lo", [P, KC, S], A0 + 32 * KB, F32R)
        hid_hi = at("hid_hi", [P, FGT, S], A0 + 32 * KB, F32R)
        hid_lo = at("hid_lo", [P, FGT, S], A0 + 32 * KB + FGT * 2 * KB, F32R)

        raw = [at(f"raw{r}", [P, SUB * P], S0 + r * 4 * KB) for r in range(2)]
        w_hi = [at(f"w_hi{r}", [P, SUB * P], S0 + (2 + r) * 4 * KB, F32R) for r in range(2)]
        w_lo = [at(f"w_lo{r}", [P, SUB * P], S0 + (4 + r) * 4 * KB, F32R) for r in range(2)]
        raw.append(at("raw2", [P, SUB * P], H0 + 16 * KB))
        w_hi.append(at("w_hi2", [P, SUB * P], H0 + 20 * KB, F32R))
        w_lo.append(at("w_lo2", [P, SUB * P], H0 + 24 * KB, F32R))
        fw_hi = [at(f"fw_hi{r}", [P, KC * P], A0 + (2 * r) * 8 * KB, F32R) for r in range(2)]
        fw_lo = [at(f"fw_lo{r}", [P, KC * P], A0 + (2 * r + 1) * 8 * KB, F32R) for r in range(2)]

        k_a = bump("k_a", [P, S])
        v_a = bump("v_a", [P, NB, P])
        tmp = bump("tmp", [P, S])
        pos_f = bump("pos_f", [P, S])
        free_top = top[0]
        top[0] = 8 * KB
        fraw = [at("fraw0", [P, KC * P], C0), at("fraw1", [P, KC * P], A0 + 32 * KB + 2 * FGT * 2 * KB)]
        assert free_top <= 8 * KB
        ident = bump("ident", [P, P])
        ones = bump("ones", [P, P])
        blk64 = bump("blk64", [P, P])
        rep = bump("rep", [ROPE, P])
        swap = bump("swap", [P, P])
        causal = bump("causal", [P, S])
        gain = bump("gain", [P, G_ALL])
        small = bump("small", [P, 64])
        cst = bump("cst", [P, 2])
        sink = bump("sink", [P, HA])
        nsink = bump("nsink", [P, HA])
        pos_q = bump("pos_q", [P, NB])
        scr0 = top[0]
        rstd_x = bump("rstd_x", [P, S])
        sq = bump("sq", [P, 2, S])
        rstd = bump("rstd", [P, S])
        end0 = top[0]
        top[0] = scr0
        p_sb = bump("p_sb", [P, 2, S])
        pt_sb = bump("pt_sb", [P, 2, S])
        top[0] = scr0
        ssum = bump("ssum", [P, S])
        hsq = bump("hsq", [P, 2, S])
        rstd_h = bump("rstd_h", [P, S])
        gate_sb = at("gate_sb", [P, S], C0 + scr0)
        up_sb = at("up_sb", [P, S], C0 + scr0 + 2 * KB)
        silu_sb = at("silu_sb", [P, S], C0 + scr0 + 4 * KB)
        top[0] = end0
        xsum = bump("xsum", [P, S])
        xsum_odd = at("xsum_odd", [P, S], C0 + scr0 + 2 * KB)
        rstd_m = at("rstd_m", [P, MEM], B0 + 60 * KB)
        pos_i = at("pos_i", [P, S], B0 + 48 * KB, I32)
        pos_qi = bump("pos_qi", [P, NB], I32)
        assert C0 + top[0] <= nc.sbuf_usable_end, (C0 + top[0], nc.sbuf_usable_end)

        invf = cst[:, 0:1]
        eps = cst[:, 1:2]

        def rstd_buf(name):
            return rstd_x if name in SECOND else rstd

        def stat(a, k):
            o = 4 + 28 * (a % 2) + 4 * k
            return small[:, o:o + 4]

        def psum(name, n):
            return ctx.enter_context(nc.psum_tensor(name, [P, n, S], F32))

        acc = psum("acc", 2)
        sc_ps = psum("sc_ps", 2)
        pt_ps = psum("pt_ps", 2)
        pv_ps = psum("pv_ps", 1)
        ss_first = psum("ss_first", 1)

        def ss_bank(name):
            return sc_ps[:, 0] if name in SECOND else ss_first[:, 0]

        SPARE = 2

        def bank(name):
            g = GROUPS[name]
            return pv_ps[:, 0] if g == SPARE else acc[:, (g - (g > SPARE)) % 2]

        x_in = [sem(f"x_in{i}") for i in range(KC // 2)]
        xg_hi_done = sem("xg_hi_done")
        sum_done = sem("sum_done")
        swapped, swap_scaled, rotated = sem("swapped"), sem("swap_scaled"), sem("rotated")
        gain_in, small_in, mem_in = sem("gain_in"), sem("small_in"), sem("mem_in")
        x_again_in = [sem(f"x_again_in{i}") for i in range(4)]
        raw_in = [sem(f"raw_in{r}") for r in range(3)]
        fraw_in = [sem(f"fraw_in{r}") for r in range(2)]
        out_sent, last_sent = sem("out_sent"), sem("last_sent")
        consts_made = sem("consts_made")
        hi_done, lo_done, slot_done, part_done = sem("hi_done"), sem("lo_done"), sem("slot_done"), sem("part_done")
        acc_free = sem("acc_free")
        xg_done, xsq_done, xsum_done, xodd_done = sem("xg_done"), sem("xsq_done"), sem("xsum_done"), sem("xodd_done")
        hsq_done, hsum_done = sem("hsq_done"), sem("hsum_done")
        sq_done, ss_done, ln_done, rstd_done, applied = (sem("sq_done"), sem("ss_done"), sem("ln_done"),
                                                         sem("rstd_done"), sem("applied"))
        rep_done, rep_copied, v_turned, v_copied = (sem("rep_done"), sem("rep_copied"), sem("v_turned"),
                                                    sem("v_copied"))
        dist_made, dist_masked, arg_made, sin_made, cos_made = (
            sem("dist_made"), sem("dist_masked"), sem("arg_made"), sem("sin_made"), sem("cos_made"))
        c_hi_done, c_split, mem_scaled, mem_hi_done, mem_split = (
            sem("c_hi_done"), sem("c_split"), sem("mem_scaled"), sem("mem_hi_done"), sem("mem_split"))
        win_hi_done, win_split, y_hi_done, y_split = (sem("win_hi_done"), sem("win_split"), sem("y_hi_done"),
                                                      sem("y_split"))
        scores_done, max_ready, exp_done, p_ready, turned, pt_ready, values_done, y_done = (
            sem("scores_done"), sem("max_ready"), sem("exp_done"), sem("p_ready"), sem("turned"), sem("pt_ready"),
            sem("values_done"), sem("y_done"))
        dve_step, pool_step = sem("dve_step"), sem("pool_step")
        h_split = sem("h_split")
        silu_done, hid_made, hid_hi_done, hid_split = (sem("silu_done"), sem("hid_made"), sem("hid_hi_done"),
                                                       sem("hid_split"))

        block = ctx.enter_context(nc.Block())

        def source(i):
            kind, at_, _ = SLOTS[i]
            if kind == "in":
                t, half = at_
                if IN_TILES[t] == "k_r":
                    return w_kr[half]
                return w_in[t - (t > IN_TILES.index("k_r")), half]
            if kind == "mem_k":
                return w_memk[at_[0], at_[1]]
            return {"mem_v": w_memv, "uq": w_uq, "uk": w_uk, "uv": w_uv, "out_a": w_outa, "out_b": w_outb}[kind][at_]

        def earlier(a):
            return a if a < N_SWA else max(N_SWA, a - 1)

        def ff_slot(g, t, r):
            return g * (2 * FGT + KC) + 2 * t + r

        def ff_bank(r):
            return (NGROUPS - 1 + r) % 2

        PAIRS = FGT + KC // 2

        def ff_loops(engine, gate_up, down):
            def group(g, n_after):
                with engine.Fori(0, FGT - 1) as t:
                    gate_up(g, t, KC)
                gate_up(g, FGT - 1, FGT)
                with engine.Fori(0, KC // 2 - 1) as t:
                    down(g, t, FGT)
                down(g, KC // 2 - 1, n_after)

            with engine.Fori(0, FG - 1) as g:
                group(g, KC)
            group(FG - 1, 0)

        def key_blocks(a):
            kind, u, v, _ = STEPS[a]
            if kind == "swa":
                return [0, 1] if u > 0 else [1]
            return list(range(v + 1 if kind == "mla" else MEM // P))

        @block.sync
        def _(sp):
            def load(slot, r, src, n):
                sp.wait_ge(lo_done, slot + NS - 1)
                sp.dma_start(fraw[r][:, 0:n * P], src).then_inc(fraw_in[r], 16)

            def load_slot(i):
                if i == THIRD:
                    sp.wait_ge(values_done, N_SWA)
                else:
                    sp.wait_ge(hi_done, SLOT_BEFORE[i] + 1)
                    sp.wait_ge(lo_done, SLOT_BEFORE[i] + 1)
                sp.dma_start(raw[PLACE[i]][:, 0:SLOTS[i][2]], source(i)).then_inc(raw_in[PLACE[i]], 16)

            sp.dma_start(raw[0][:], source(0)).then_inc(raw_in[0], 16)
            for c in range(KC // 2):
                sp.dma_start(x_sb[:, 2 * c:2 * c + 2], xT[:, 2 * c:2 * c + 2]).then_inc(x_in[c], 16)
                if c == 0:
                    sp.dma_start(gain[:], gains).then_inc(gain_in, 16)
                if c == 2:
                    sp.dma_start(raw[1][:], source(1)).then_inc(raw_in[1], 16)
                if c == 5:
                    load_slot(2)
            for stage, i in plan:
                if stage == "split" and i > 2:
                    load_slot(i)
                    if i == 3:
                        sp.dma_start(pos_i[:], pos_rows).then_inc(small_in, 16)
                        sp.dma_start(pos_qi[:], pos_cols).then_inc(small_in, 16)
                        sp.dma_start(sink[:], sink_rows).then_inc(small_in, 16)
                        sp.dma_start(invf, inv_freq).then_inc(small_in, 16)
                elif stage == "mem_load":
                    sp.wait_ge(xg_done, KC)
                    sp.wait_ge(xsq_done, KC)
                    sp.dma_start(mem_raw[:], memT).then_inc(mem_in, 16)
                elif stage == "first_ff_load":
                    sp.wait_ge(values_done, N_SWA)
                    sp.wait_ge(rotated, 3)
                    sp.dma_start(fraw[0][:], w_gu[0]).then_inc(fraw_in[0], 16)
                elif stage == "x_again":
                    if i < 2:
                        sp.wait_ge(mem_split, 4)
                    else:
                        sp.wait_ge(slot_done, SLOTS_UV)
                        sp.wait_ge(rotated, 3)
                    sp.dma_start(h_sb[:, 4 * i:4 * i + 4], xT[:, 4 * i:4 * i + 4]).then_inc(x_again_in[i], 16)

            def gate_up(g, first):
                with sp.Fori(first, FGT) as t:
                    for r in range(2):
                        load(ff_slot(g, t, r), r, w_gu[(g * FGT + t) * 2 + r], KC)

            def down(g):
                with sp.Fori(0, KC // 2) as t:
                    for r in range(2):
                        load(ff_slot(g, t + FGT, r), r, w_dn[g * KC + t * 2 + r], FGT)

            sp.wait_ge(slot_done, NS)
            load(1, 1, w_gu[1], KC)
            gate_up(0, 1)
            down(0)
            with sp.Fori(1, FG) as g:
                gate_up(g, 0)
                down(g)
            for m in (KC - 2, KC - 1):
                sp.wait_ge(acc_free, NGROUPS + ff_slot(FG - 1, FGT + m // 2, m % 2) + 1)
                sp.dma_start(outT[:, m], h_sb[:, m]).then_inc(last_sent, 16)
            sp.wait_ge(last_sent, 32)

        @block.tensor
        def _(pe):
            mm = nc.tensor.matmul

            def three(out, hi, lo, x_hi, x_lo, start, stop):
                mm(out, hi, x_hi, start=start, stop=False)
                mm(out, hi, x_lo, start=False, stop=False)
                return mm(out, lo, x_hi, start=False, stop=stop)

            def open_group(name):
                g = GROUPS[name]
                if g > SPARE:
                    pe.wait_ge(acc_free, g - 1 - (g <= SPARE + 2))

            def slot(i, first=0, end=SUB):
                kind, at_, _ = SLOTS[i]
                hi, lo = w_hi[PLACE[i]], w_lo[PLACE[i]]
                if first == 0:
                    pe.wait_ge(hi_done, i + 1)
                    pe.wait_ge(lo_done, i + 1)
                if kind == "in":
                    t, half = at_
                    name = IN_TILES[t]
                    m = ROPE if name == "k_r" else P
                    if half == 0:
                        open_group(name)
                    for k in range(SUB):
                        c = half * SUB + k
                        if t == 0:
                            pe.wait_ge(xg_done, c + 1)
                        last = three(bank(name)[0:m], hi[:, k * m:(k + 1) * m], lo[:, k * m:(k + 1) * m],
                                     xg_hi[:, c], xg_lo[:, c], c == 0, c == KC - 1)
                elif kind == "mem_k":
                    h, half = at_
                    name = (kind, h)
                    if half == 0:
                        open_group(name)
                    for k in range(SUB):
                        c = half * SUB + k
                        if h == 0 and c % 4 == 0:
                            pe.wait_ge(mem_split, c // 4 + 1)
                        last = three(bank(name)[:, 0:MEM], hi[:, k * P:(k + 1) * P], lo[:, k * P:(k + 1) * P],
                                     mem_hi[:, c], mem_lo[:, c], c == 0, c == KC - 1)
                elif kind == "mem_v":
                    for t in range(MEM // P):
                        name = (kind, t)
                        if at_ == 0:
                            open_group(name)
                        for k in range(2):
                            c = 2 * at_ + k
                            rows = slice(t * P, (t + 1) * P)
                            out = bank(name)
                            wh, wl = hi[:, k * S:(k + 1) * S], lo[:, k * S:(k + 1) * S]
                            mm(out, mem_hi[:, c, rows], wh, start=c == 0, stop=False)
                            mm(out, mem_hi[:, c, rows], wl, start=False, stop=False)
                            last = mm(out, mem_lo[:, c, rows], wh, start=False, stop=c == KC - 1)
                        if (at_, t) == (KC // 2 - 1, 0):
                            last.then_inc(part_done, 1)
                elif kind in ("uq", "uk"):
                    off = 0 if kind == "uq" else 4
                    for j in range(2):
                        name = (kind, 2 * at_ + j)
                        open_group(name)
                        if name == ("uq", 0):
                            pe.wait_ge(c_split, 8)
                        for c in range(4):
                            k = j * 4 + c
                            last = three(bank(name), hi[:, k * P:(k + 1) * P], lo[:, k * P:(k + 1) * P],
                                         c_hi[:, off + c], c_lo[:, off + c], c == 0, c == 3)
                        if j == 0:
                            last.then_inc(part_done, 1)
                elif kind == "uv":
                    for t in range(NB):
                        name = (kind, 4 * at_ + t)
                        open_group(name)
                        rows = slice(t * P, (t + 1) * P)
                        for c in range(4):
                            out = bank(name)[:, 0:2 * P]
                            wh, wl = hi[:, c * 2 * P:(c + 1) * 2 * P], lo[:, c * 2 * P:(c + 1) * 2 * P]
                            mm(out, c_hi[:, 4 + c, rows], wh, start=c == 0, stop=False)
                            mm(out, c_hi[:, 4 + c, rows], wl, start=False, stop=False)
                            last = mm(out, c_lo[:, 4 + c, rows], wh, start=False, stop=c == 3)
                        if t < NB - 1:
                            last.then_inc(part_done, 1)
                else:
                    off = 0 if kind == "out_a" else SUB
                    name = (kind, at_)
                    if first == 0:
                        open_group(name)
                    for k in range(first, end):
                        if name == ("out_a", 0):
                            pe.wait_ge(win_split, k + 1)
                        if kind == "out_b" and at_ < 2:
                            pe.wait_ge(y_split, k + 1)
                        last = three(bank(name), hi[:, k * P:(k + 1) * P], lo[:, k * P:(k + 1) * P],
                                     y_hi[:, off + k], y_lo[:, off + k], k == 0, k == SUB - 1)
                if end == SUB:
                    last.then_inc(slot_done, 1)

            def sum_squares(name, k, n):
                if k == 0 and norm_before(name, False):
                    pe.wait_ge(rstd_done, NORM_AT[norm_before(name, False)])
                elif name in SECOND:
                    pe.wait_ge(p_ready, N_SWA)
                ss_ps = ss_bank(name)
                if name == "x":
                    pe.wait_ge(consts_made, 1)
                    pe.wait_ge(xsum_done, KC // 2)
                    pe.wait_ge(xodd_done, KC // 2)
                    src = xsum[:]
                    mm(ss_ps, ones[:], xsum_odd[:], start=True, stop=False)
                elif name == "h":
                    pe.wait_ge(hsum_done, KC)
                    src = ssum[:]
                elif (name, k) in SUM_AT:
                    pe.wait_ge(sum_done, SUM_END[name])
                    src = xsum[:]
                else:
                    pe.wait_ge(sq_done, SQ_AT[(name, k)])
                    src = sq[:, (SQ_AT[(name, k)] - 1) % 2]
                if name in ("k_a", "k_r", ("uq", 4), ("uq", 5)) or str(name).startswith("q_a"):
                    group = blk64
                else:
                    group = ones
                if name == "mem":
                    mm(ss_ps[:, 0:MEM], group[:], src[:, 0:MEM], start=True, stop=False)
                    mm(ss_ps[:, 0:MEM], group[:], src[:, MEM:], start=False, stop=True).then_inc(ss_done, 1)
                elif name[0] == "mem_k":
                    mm(ss_ps[:, 0:MEM], group[:], src[:, 0:MEM], start=True, stop=True).then_inc(ss_done, 1)
                else:
                    mm(ss_ps, group[:], src, start=k == 0 and name != "x", stop=k == n - 1).then_inc(ss_done, 1)

            def scores(a):
                kind, u, v, r = STEPS[a]
                if a > 0:
                    pe.wait_ge(p_ready, earlier(a))
                if kind == "swa":
                    b, g = u, v
                    pe.wait_ge(applied, APPLY_AT[f"q_a{4 * r + 3}"])
                    rows = slice(g * DA, (g + 1) * DA)
                    k0 = 0 if b else P
                    for j in range(4):
                        c0 = (j % 2) * 2 * P
                        last = mm(sc_ps[:, j // 2, c0 + k0:c0 + 2 * P],
                                  q_a[rows, 4 * r + j, b * P:(b + 1) * P],
                                  k_a[rows, (b - 1) * P + k0:(b + 1) * P], start=True, stop=True)
                elif kind == "mla":
                    h, q = u, v
                    pe.wait_ge(applied, APPLY_AT[("uk", 3)])
                    pe.wait_ge(rotated, 3)
                    pe.wait_ge(acc_free, GROUPS[("uv", 7)] + 1)
                    n = (q + 1) * P
                    out, qs = sc_ps[:, a % 2, 0:n], slice(q * P, (q + 1) * P)
                    mm(out, q_b[:, h, qs], k_b[:, h, 0:n], start=True, stop=False)
                    rows = slice(ROPE * (h % 2), ROPE * (h % 2) + ROPE)
                    last = mm(out, q_rt[rows, h // 2, qs], k_rt[rows, 0:n], start=False, stop=True)
                else:
                    h, q = u, v
                    last = mm(sc_ps[:, a % 2, 0:MEM], q_m[:, h, q * P:(q + 1) * P], k_m[:, h], start=True, stop=True)
                last.then_inc(scores_done, 1)

            def turn(a):
                kind = STEPS[a][0]
                pe.wait_ge(p_ready, a + 1)
                if a > 0:
                    pe.wait_ge(pt_ready, earlier(a))
                for kb in key_blocks(a):
                    if kind == "swa":
                        for j in range(4):
                            last = nc.tensor.transpose(pt_ps[:, kb, j * P:(j + 1) * P],
                                                       win_p[:, j, kb * P:(kb + 1) * P], ident[:])
                    else:
                        last = nc.tensor.transpose(pt_ps[:, a % 2, kb * P:(kb + 1) * P],
                                                   p_sb[:, a % 2, kb * P:(kb + 1) * P], ident[:])
                last.then_inc(turned, 1)

            def values(a):
                kind, u, v, r = STEPS[a]
                pe.wait_ge(pt_ready, a + 1)
                kbs = key_blocks(a)
                if kind == "swa":
                    b, g = u, v
                    if a > 0:
                        pe.wait_ge(y_done, a)
                    for kb in kbs:
                        last = mm(pv_ps[g * DA:(g + 1) * DA, 0], v_a[:, b - 1 + kb, g * DA:(g + 1) * DA],
                                  win_pt[:, kb], start=kb == kbs[0], stop=kb == kbs[-1])
                else:
                    head, q = (a - N_SWA) // NB, v
                    if q == 0:
                        pe.wait_ge(y_done, N_SWA)
                        if head >= 1:
                            pe.wait_ge(y_split, head)
                    vals = v_b if kind == "mla" else v_m
                    for kb in kbs:
                        last = mm(pv_ps[:, 0, q * P:(q + 1) * P], vals[:, kb, u * P:(u + 1) * P],
                                  pt_sb[:, a % 2, kb * P:(kb + 1) * P], start=kb == kbs[0], stop=kb == kbs[-1])
                last.then_inc(values_done, 1)

            def tile(r, s_, n, x_hi, x_lo, hidden=None, first=False):
                pe.wait_ge(lo_done, NS + s_ + 1)
                if first:
                    pe.wait_ge(acc_free, NGROUPS - 1)
                for k in range(n):
                    if hidden is not None and k >= n - 2:
                        pe.wait_ge(hid_split, hidden + k + 1)
                    if first:
                        pe.wait_ge(h_split, k + 1)
                    last = three(acc[:, ff_bank(r)], fw_hi[r][:, k * P:(k + 1) * P], fw_lo[r][:, k * P:(k + 1) * P],
                                 x_hi[:, k], x_lo[:, k], k == 0, k == n - 1)
                last.then_inc(slot_done, 1)

            turns_made = 0
            rep_seen = False
            for stage, i in plan:
                if stage == "slot":
                    slot(i)
                elif stage == "slot_part":
                    slot(*i)
                elif stage == "ss":
                    sum_squares(*i)
                elif stage == "v_turn":
                    pe.wait_ge(consts_made, 1)
                    pe.wait_ge(acc_free, GROUPS["v_a"] + 1)
                    for b in range(NB):
                        last = nc.tensor.transpose(pt_ps[:, 0, b * P:(b + 1) * P], tmp[:, b * P:(b + 1) * P], ident[:])
                    last.then_inc(v_turned, 1)
                elif stage == "rep":
                    pe.wait_ge(acc_free, GROUPS["k_r"] + 1)
                    pe.wait_ge(pt_ready, turns_made)
                    mm(pt_ps[:, 0], rep[:], tmp[0:ROPE], start=True, stop=True).then_inc(rep_done, 1)
                    rep_seen = True
                elif stage == "swap":
                    pe.wait_ge(applied, APPLY_AT["k_r" if i == 0 else ("uq", 3 + i)])
                    pe.wait_ge(pt_ready, N_SWA)
                    if i:
                        pe.wait_ge(swap_scaled, 1)
                    src = k_rt[:] if i == 0 else q_rt[:, i - 1]
                    mm(pt_ps[:, i % 2], swap[:], src, start=True, stop=True).then_inc(swapped, 1)
                elif stage == "scores":
                    scores(i)
                elif stage == "turn":
                    if i == 0:
                        pe.wait_ge(v_copied, 1)
                    if rep_seen:
                        pe.wait_ge(rep_copied, 1)
                    turn(i)
                    turns_made += 1
                elif stage == "values":
                    values(i)
                elif stage == "first_ff_tile":
                    tile(0, 0, KC, f_hi, f_lo, first=True)

            def group(g, first):
                with pe.Fori(first, FGT) as t:
                    for r in range(2):
                        tile(r, ff_slot(g, t, r), KC, f_hi, f_lo)
                with pe.Fori(0, KC // 2) as t:
                    for r in range(2):
                        tile(r, ff_slot(g, t + FGT, r), FGT, hid_hi, hid_lo, g * FGT)

            tile(1, 1, KC, f_hi, f_lo)
            group(0, 1)
            with pe.Fori(1, FG) as g:
                group(g, 0)

        @block.scalar
        def _(act):
            A = nc.scalar

            def sq_source(name, k):
                if name in ("k_a", "k_r"):
                    return k_a[:] if name == "k_a" else k_rt[:]
                if name[0] == "uq":
                    return q_b[:, name[1]] if name[1] < 4 else q_rt[:, name[1] - 4]
                if name[0] == "uk":
                    return k_b[:, name[1]]
                if name == "c_q":
                    return q_b[:, k]
                if name == "c_kv":
                    return k_b[:, k]
                return q_a[:, int(name[-1])] if name.startswith("q_a") else q_m[:, int(name[-1])]

            def evacuated(name, k):
                if name in ("c_q", "c_kv"):
                    return GROUPS[f"{name}{k}"] + 1
                return GROUPS[name] + 1

            def split_ff(s_, pair, r, n):
                act.wait_ge(fraw_in[r], 16 * (pair + 1))
                act.wait_ge(slot_done, NS + s_ - 1)
                A.activation(fw_hi[r][:, 0:n * P], fraw[r][:, 0:n * P], ACT.Copy).then_inc(hi_done, 1)

            A.preload_act_table_set(LN_EXP_SET)
            for stage, i in plan:
                if stage == "split":
                    act.wait_ge(raw_in[PLACE[i]], 16 * USE[i])
                    if SLOT_BEFORE[i] is not None:
                        act.wait_ge(slot_done, SLOT_BEFORE[i] + 1)
                    n, r = SLOTS[i][2], PLACE[i]
                    A.activation(w_hi[r][:, 0:n], raw[r][:, 0:n], ACT.Copy).then_inc(hi_done, 1)
                elif stage == "x_pair":
                    if i == 0:
                        act.wait_ge(gain_in, 16)
                    act.wait_ge(x_in[i], 16)
                    for c in (2 * i, 2 * i + 1):
                        A.activation(xg_hi[:, c], x_sb[:, c], ACT.Copy,
                                     scale=gain[:, G_ATT + c:G_ATT + c + 1]).then_inc(xg_hi_done, 1)
                elif stage == "x_sq":
                    A.activation(x_sq[:, i], x_sb[:, i], ACT.Square).then_inc(xsq_done, 1)
                elif stage == "sines":
                    act.wait_ge(arg_made, 1)
                    A.activation(sin[:], ang[:], ACT.Sin).then_inc(sin_made, 1)
                    A.activation(cos[:], ang[:], ACT.Sin, scale=0.5).then_inc(sin_made, 1)
                    A.preload_act_table_set(LN_EXP_SET)
                elif stage == "sq":
                    name, k = i
                    n = SQ_AT[i]
                    if n <= 2:
                        act.wait_ge(ss_done, SS_END["x"])
                    elif n - 2 in SUM_OF_SQ:
                        act.wait_ge(sum_done, SUM_OF_SQ[n - 2])
                    else:
                        act.wait_ge(ss_done, SS_OF_SQ[n - 2])
                    if name == "mem":
                        act.wait_ge(mem_in, 16)
                        src = mem_raw[:, 2 * k:2 * k + 2].rearrange("p c m -> p (c m)")
                        A.activation(sq[:, (n - 1) % 2], src, ACT.Square).then_inc(sq_done, 1)
                    elif name[0] == "mem_k":
                        act.wait_ge(acc_free, GROUPS[name] + 1)
                        A.activation(sq[:, (n - 1) % 2, 0:MEM], k_m[:, name[1]], ACT.Square).then_inc(sq_done, 1)
                    else:
                        if name == "k_r":
                            act.wait_ge(rep_copied, 1)
                        else:
                            act.wait_ge(acc_free, evacuated(name, k))
                        A.activation(sq[:, (n - 1) % 2], sq_source(name, k), ACT.Square).then_inc(sq_done, 1)
                elif stage == "first_ff_split":
                    act.wait_ge(fraw_in[i], 16)
                    act.wait_ge(slot_done, NS if i else NS - KC)
                    A.activation(fw_hi[i][:], fraw[i][:], ACT.Copy).then_inc(hi_done, 1)
                elif stage == "rstd":
                    j = NORM_AT[i]
                    n_sum = {"x": D, "h": D, "mem": D, "k_a": DA, "c_q": RANK, "c_kv": RANK, "k_r": ROPE,
                             ("uq", 4): ROPE, ("uq", 5): ROPE}.get(i, DA if str(i).startswith("q_a") else P)
                    w = MEM if i == "mem" or i[0] == "mem_k" else S
                    ss_ps = ss_bank(i)
                    act.wait_ge(ss_done, SS_END[i])
                    A.activation(ss_ps[:, 0:w], ss_ps[:, 0:w], ACT.Ln, bias=eps,
                                 scale=1.0 / n_sum).then_inc(ln_done, 1)
                    act.wait_ge(ln_done, j)
                    if i not in ("x", "mem", "h") and norm_before(i, True):
                        act.wait_ge(applied, APPLY_AT[norm_before(i, True)])
                    elif i in SECOND:
                        act.wait_ge(acc_free, GROUPS["q_m3"] + 1)
                    if i == "h":
                        act.wait_ge(values_done, N_STEPS)
                    dst = {"x": rstd_x, "h": rstd_h, "mem": rstd_m}.get(i, rstd_buf(i))
                    A.activation(dst[:, 0:w], ss_ps[:, 0:w], ACT.Exp, scale=-0.5).then_inc(rstd_done, 1)
                elif stage == "v_turn":
                    act.wait_ge(v_turned, 1)
                    A.activation(v_a[:].rearrange("p b d -> p (b d)"), pt_ps[:, 0], ACT.Copy).then_inc(v_copied, 1)
                elif stage == "rep":
                    act.wait_ge(rep_done, 1)
                    A.activation(k_rt[:], pt_ps[:, 0], ACT.Copy).then_inc(rep_copied, 1)
                elif stage == "mem_split":
                    act.wait_ge(mem_scaled, i + 1)
                    act.wait_ge(slot_done, SLOTS_IN - 1)
                    A.activation(mem_hi[:, 4 * i:4 * i + 4], mem_raw[:, 4 * i:4 * i + 4],
                                 ACT.Copy).then_inc(mem_hi_done, 1)
                elif stage == "c_split":
                    if i == 0:
                        act.wait_ge(applied, APPLY_AT["c_kv"])
                        act.wait_ge(slot_done, SLOTS_IN)
                    src = q_b[:, i] if i < 4 else k_b[:, i - 4]
                    A.activation(c_hi[:, i], src, ACT.Copy).then_inc(c_hi_done, 1)
                elif stage == "window_split":
                    if i == 0:
                        act.wait_ge(slot_done, SLOTS_MEM)
                        act.wait_ge(y_done, N_SWA)
                    A.activation(y_hi[:, i], q_a[:, i], ACT.Copy).then_inc(win_hi_done, 1)
                elif stage == "softmax":
                    kind, u, v, r = STEPS[i]
                    act.wait_ge(max_ready, i + 1)
                    if i == N_SWA:
                        act.wait_ge(applied, APPLY_AT[("uk", 3)])
                    nmax, sums = stat(i, 1), stat(i, 2)
                    if kind == "swa":
                        k0 = 0 if u else P
                        A.activation(stat(i, 4), stat(i, 3), ACT.Exp)
                        for j in range(4):
                            ins = A.activation(win_p[:, j, k0:], win_p[:, j, k0:], ACT.Exp, bias=nmax[:, j:j + 1],
                                               scale=DA ** -0.5, accum_out=sums[:, j:j + 1])
                        ins.then_inc(exp_done, 1)
                    elif kind == "mla":
                        w = (v + 1) * P
                        A.activation(p_sb[:, i % 2, 0:w], p_sb[:, i % 2, 0:w], ACT.Exp, bias=nmax[:, 0:1],
                                     scale=(NOPE + ROPE) ** -0.5, accum_out=sums[:, 0:1]).then_inc(exp_done, 1)
                    else:
                        if i >= N_SWA + 2:
                            act.wait_ge(turned, i - 1)
                        A.activation(p_sb[:, i % 2, 0:MEM], sc_ps[:, i % 2, 0:MEM], ACT.Exp, bias=nmax[:, 0:1],
                                     scale=P ** -0.5, accum_out=sums[:, 0:1]).then_inc(exp_done, 1)
                elif stage == "turn":
                    kind = STEPS[i][0]
                    act.wait_ge(turned, i + 1)
                    if i > 0:
                        act.wait_ge(values_done, earlier(i))
                    kbs = key_blocks(i)
                    if kind == "swa":
                        for kb in kbs:
                            ins = A.activation(win_pt[:, kb], pt_ps[:, kb], ACT.Copy)
                    else:
                        w = len(kbs) * P
                        ins = A.activation(pt_sb[:, i % 2, 0:w], pt_ps[:, i % 2, 0:w], ACT.Copy)
                    ins.then_inc(pt_ready, 1)
                elif stage == "values" and i >= N_SWA and STEPS[i][2] == NB - 1:
                    head = (i - N_SWA) // NB
                    act.wait_ge(values_done, i + 1)
                    act.wait_ge(slot_done, SLOTS_UV)
                    A.activation(y_hi[:, 8 + head], pv_ps[:, 0], ACT.Copy).then_inc(y_hi_done, 1)
                elif stage == "h_tile":
                    act.wait_ge(acc_free, GROUPS[("out_b", i)] + 1)
                    act.wait_ge(values_done, N_STEPS)
                    if i >= 2:
                        act.wait_ge(hsum_done, i - 1)
                    A.activation(hsq[:, i % 2], h_sb[:, i], ACT.Square).then_inc(hsq_done, 1)

            def gate_up(g, t, n_next):
                pair = g * PAIRS + t
                split_ff(ff_slot(g, t, 2), pair + 1, 0, n_next)
                act.wait_ge(acc_free, NGROUPS + ff_slot(g, t, 0) + 1)
                A.activation(silu_sb[:], gate_sb[:], ACT.Silu).then_inc(silu_done, 1)
                split_ff(ff_slot(g, t, 3), pair + 1, 1, n_next)
                act.wait_ge(hid_made, g * FGT + t + 1)
                A.activation(hid_hi[:, t], up_sb[:], ACT.Copy).then_inc(hid_hi_done, 1)

            def down(g, t, n_next):
                for r in range(2 if n_next else 0):
                    split_ff(ff_slot(g, t + FGT, 2 + r), g * PAIRS + FGT + t + 1, r, n_next)

            A.preload_act_table(ACT.Silu)
            ff_loops(act, gate_up, down)

        @block.vector
        def _(dve):
            V = nc.vector
            chain = [0]

            def link(ins):
                chain[0] += 1
                ins.then_inc(dve_step, 1)
                dve.wait_ge(dve_step, chain[0])

            def gained(name, k=0):
                if name == "k_a":
                    return k_a[:], G_KA
                if name == "k_r":
                    return k_rt[:], G_KR
                if name == "c_q":
                    return q_b[:, k], G_CQ + k
                if name == "c_kv":
                    return k_b[:, k], G_CKV + k
                if name[0] == "uq":
                    return (q_b[:, name[1]], G_QN) if name[1] < 4 else (q_rt[:, name[1] - 4], G_QR)
                if name[0] == "uk":
                    return k_b[:, name[1]], G_KN
                if name[0] == "mem_k":
                    return k_m[:, name[1]], G_KM
                if name.startswith("q_a"):
                    return q_a[:, int(name[-1])], G_QA
                return q_m[:, int(name[-1])], G_QM

            def apply_norm(name):
                j = NORM_AT[name]
                dve.wait_ge(rstd_done, j)
                n = {"c_q": 4, "c_kv": 4}.get(name, 1)
                w = MEM if name[0] == "mem_k" else S
                for k in range(n):
                    t, c = gained(name, k)
                    ins = V.scalar_tensor_tensor(t, t, gain[:, c:c + 1], rstd_buf(name)[:, 0:w], ALU.mult, ALU.mult)
                ins.then_inc(applied, 1)

            def evacuate(name):
                ends_slot, n = GROUP_ENDS[name]
                dve.wait_ge(slot_done if ends_slot else part_done, n)
                src = bank(name)
                if name in IN_TILES:
                    if name == "k_a":
                        dve.wait_ge(rstd_done, NORM_AT["x"])
                    if name == "k_r":
                        dve.wait_ge(v_turned, 1)
                        ins = V.tensor_tensor(tmp[0:ROPE], src[0:ROPE], rstd_x[0:ROPE], ALU.mult)
                    else:
                        dst = {"k_a": k_a[:], "v_a": tmp[:]}.get(name)
                        if dst is None:
                            buf = {"q_a": q_a, "c_q": q_b, "c_k": k_b, "q_m": q_m}[name[:3]]
                            dst = buf[:, int(name[-1])]
                        ins = V.tensor_tensor(dst, src, rstd_x[:], ALU.mult)
                elif name[0] == "mem_k":
                    ins = V.tensor_copy(k_m[:, name[1]], src[:, 0:MEM])
                elif name[0] == "mem_v":
                    ins = V.tensor_copy(v_m[:, name[1]], src)
                elif name[0] == "uq":
                    ins = V.tensor_copy(q_b[:, name[1]] if name[1] < 4 else q_rt[:, name[1] - 4], src)
                elif name[0] == "uk":
                    ins = V.tensor_copy(k_b[:, name[1]], src)
                elif name[0] == "uv":
                    s_, t = divmod(name[1], 4)
                    ins = V.tensor_copy(v_b[:, t, s_ * 2 * P:(s_ + 1) * 2 * P], src[:, 0:2 * P])
                else:
                    if name[0] == "out_a" and name[1] % 4 == 0:
                        dve.wait_ge(x_again_in[name[1] // 4], 16)
                    ins = V.tensor_tensor(h_sb[:, name[1]], src, h_sb[:, name[1]], ALU.add)
                ins.then_inc(acc_free, 1)

            def softmax(a):
                kind, u, v, r = STEPS[a]
                dve.wait_ge(scores_done, a + 1)
                mx, nmax = stat(a, 0), stat(a, 1)
                if kind == "swa":
                    b, g = u, v
                    k0 = 0 if b else P
                    if a == 0:
                        dve.wait_ge(dist_masked, NB)
                        dve.wait_ge(cos_made, 1)
                    else:
                        dve.wait_ge(turned, a)
                    for j in range(4):
                        slope = 2.0 ** (-8.0 * (g * 8 + 4 * r + j + 1) / HA)
                        c0 = (j % 2) * 2 * P
                        ins = V.scalar_tensor_tensor(win_p[:, j, k0:], dist[:, b, k0:], -slope * DA ** 0.5,
                                                     sc_ps[:, j // 2, c0 + k0:c0 + 2 * P], ALU.mult, ALU.add)
                    link(ins)
                    link(V.tensor_reduce(mx, win_p[:, :, k0:], AX.X, ALU.max))
                    heads = slice(g * 8 + 4 * r, g * 8 + 4 * r + 4)
                    link(V.scalar_tensor_tensor(nmax, mx, -DA ** -0.5, nsink[:, heads], ALU.mult, ALU.min))
                    V.tensor_tensor(stat(a, 3), sink[:, heads], nmax, ALU.add).then_inc(max_ready, 1)
                elif kind == "mla":
                    w = (v + 1) * P
                    if a >= N_SWA + 2:
                        dve.wait_ge(turned, a - 1)
                    else:
                        dve.wait_ge(applied, APPLY_AT[("uk", 3)])
                    link(V.tensor_tensor(p_sb[:, a % 2, 0:w], sc_ps[:, a % 2, 0:w],
                                         causal[:, S - w:], ALU.add))
                    link(V.tensor_reduce(mx[:, 0:1], p_sb[:, a % 2, 0:w], AX.X, ALU.max))
                    V.tensor_scalar(nmax[:, 0:1], mx[:, 0:1], -(NOPE + ROPE) ** -0.5, None,
                                    ALU.mult).then_inc(max_ready, 1)
                else:
                    link(V.tensor_reduce(mx[:, 0:1], sc_ps[:, a % 2, 0:MEM], AX.X, ALU.max))
                    V.tensor_scalar(nmax[:, 0:1], mx[:, 0:1], -P ** -0.5, None, ALU.mult).then_inc(max_ready, 1)

            def p_norm(a):
                kind, u, v, r = STEPS[a]
                dve.wait_ge(exp_done, a + 1)
                sums, rec = stat(a, 2), stat(a, 6)
                if kind == "swa":
                    k0 = 0 if u else P
                    den = stat(a, 5)
                    link(V.tensor_tensor(den, sums, stat(a, 4), ALU.add))
                    link(V.reciprocal(rec, den))
                    for j in range(4):
                        ins = V.tensor_scalar(win_p[:, j, k0:], win_p[:, j, k0:], rec[:, j:j + 1], None, ALU.mult)
                else:
                    w = len(key_blocks(a)) * P
                    link(V.reciprocal(rec[:, 0:1], sums[:, 0:1]))
                    ins = V.tensor_scalar(p_sb[:, a % 2, 0:w], p_sb[:, a % 2, 0:w], rec[:, 0:1], None, ALU.mult)
                ins.then_inc(p_ready, 1)

            def split_ff(s_, r, n):
                dve.wait_ge(hi_done, NS + s_ + 1)
                V.tensor_tensor(fw_lo[r][:, 0:n * P], fraw[r][:, 0:n * P], fw_hi[r][:, 0:n * P].bitcast(F32),
                                ALU.subtract).then_inc(lo_done, 1)

            for stage, i in plan:
                if stage == "first_ff_split":
                    split_ff(i, i, KC)
                elif stage == "split":
                    n = SLOTS[i][2]
                    dve.wait_ge(hi_done, i + 1)
                    r = PLACE[i]
                    V.tensor_tensor(w_lo[r][:, 0:n], raw[r][:, 0:n], w_hi[r][:, 0:n].bitcast(F32),
                                    ALU.subtract).then_inc(lo_done, 1)
                elif stage == "x_pair":
                    for c in (2 * i, 2 * i + 1):
                        dve.wait_ge(xg_hi_done, c + 1)
                        V.scalar_tensor_tensor(xg_lo[:, c], x_sb[:, c], gain[:, G_ATT + c:G_ATT + c + 1],
                                               xg_hi[:, c].bitcast(F32), ALU.mult, ALU.subtract).then_inc(xg_done, 1)
                elif stage == "x_sq" and i % 2:
                    dve.wait_ge(xsq_done, i + 1)
                    if i == 1:
                        V.tensor_copy(xsum_odd[:], x_sq[:, i]).then_inc(xodd_done, 1)
                    else:
                        dve.wait_ge(xodd_done, i // 2)
                        V.tensor_tensor(xsum_odd[:], xsum_odd[:], x_sq[:, i], ALU.add).then_inc(xodd_done, 1)
                elif stage == "setup":
                    dve.wait_ge(small_in, 64)
                    dve.wait_ge(xsq_done, KC)
                    V.tensor_copy(pos_f[:], pos_i[:])
                    V.tensor_scalar(nsink[:], sink[:], -1.0, None, ALU.mult)
                    link(V.tensor_copy(pos_q[:], pos_qi[:]))
                    for b in range(NB):
                        k0 = 0 if b else P
                        link(V.tensor_scalar(dist[:, b, k0:], pos_f[:, (b - 1) * P + k0:(b + 1) * P],
                                             pos_q[:, b:b + 1], None, ALU.subtract))
                        V.scalar_tensor_tensor(dist[:, b, k0:], dist[:, b, k0:], -1.0, dist[:, b, k0:], ALU.mult,
                                               ALU.max).then_inc(dist_made, 1)
                elif stage == "angles":
                    link(V.tensor_scalar(ang[:], pos_f[:], invf, None, ALU.mult))
                    link(V.tensor_scalar(turns[:], ang[:], 1.0 / TWO_PI, MAGIC, ALU.mult, ALU.add))
                    link(V.tensor_scalar(turns[:], turns[:], -MAGIC, None, ALU.add))
                    for part in (C1, C2, C3):
                        link(V.scalar_tensor_tensor(ang[:], turns[:], -part, ang[:], ALU.mult, ALU.add))
                    V.tensor_scalar(ang[:], ang[:], 3.1415925, -3.1415925, ALU.min, ALU.max).then_inc(arg_made, 1)
                elif stage == "sines":
                    dve.wait_ge(sin_made, 2)
                    link(V.tensor_tensor(cos[:], cos[:], cos[:], ALU.mult))
                    V.tensor_scalar(cos[:], cos[:], -2.0, 1.0, ALU.mult, ALU.add).then_inc(cos_made, 1)
                elif stage == "apply":
                    apply_norm(i)
                elif stage == "evac":
                    evacuate(i)
                elif stage == "swap":
                    dve.wait_ge(swapped, i + 1)
                    dve.wait_ge(cos_made, 1)
                    if i == 1:
                        dve.wait_ge(rotated, 1)
                    V.tensor_tensor(tmp[:] if i < 2 else pos_f[:], pt_ps[:, i % 2], sin[:],
                                    ALU.mult).then_inc(swap_scaled, 1)
                elif stage == "mem_scale":
                    dve.wait_ge(rstd_done, NORM_AT["mem"])
                    for c in range(4 * i, 4 * i + 4):
                        ins = V.scalar_tensor_tensor(mem_raw[:, c], mem_raw[:, c], gain[:, G_MEM + c:G_MEM + c + 1],
                                                     rstd_m[:], ALU.mult, ALU.mult)
                    ins.then_inc(mem_scaled, 1)
                elif stage == "mem_split":
                    dve.wait_ge(mem_hi_done, i + 1)
                    V.tensor_tensor(mem_lo[:, 4 * i:4 * i + 4], mem_raw[:, 4 * i:4 * i + 4],
                                    mem_hi[:, 4 * i:4 * i + 4].bitcast(F32), ALU.subtract).then_inc(mem_split, 1)
                elif stage == "c_split":
                    dve.wait_ge(c_hi_done, i + 1)
                    src = q_b[:, i] if i < 4 else k_b[:, i - 4]
                    V.tensor_tensor(c_lo[:, i], src, c_hi[:, i].bitcast(F32), ALU.subtract).then_inc(c_split, 1)
                elif stage == "window_split":
                    dve.wait_ge(win_hi_done, i + 1)
                    V.tensor_tensor(y_lo[:, i], q_a[:, i], y_hi[:, i].bitcast(F32), ALU.subtract).then_inc(win_split, 1)
                elif stage == "softmax":
                    softmax(i)
                elif stage == "p_norm":
                    p_norm(i)
                elif stage == "values":
                    kind, u, v, r = STEPS[i]
                    if kind == "swa":
                        dve.wait_ge(values_done, i + 1)
                        rows = slice(v * DA, (v + 1) * DA)
                        V.tensor_copy(q_a[rows, 4 * r:4 * r + 4, u * P:(u + 1) * P],
                                      pv_ps[rows, 0].rearrange("p (h q) -> p h q", h=4)).then_inc(y_done, 1)
                    elif v == NB - 1:
                        head = (i - N_SWA) // NB
                        dve.wait_ge(y_hi_done, head + 1)
                        V.tensor_tensor(y_lo[:, 8 + head], pv_ps[:, 0], y_hi[:, 8 + head].bitcast(F32),
                                        ALU.subtract).then_inc(y_split, 1)
                elif stage == "h_tile":
                    if i == 0:
                        dve.wait_ge(values_done, N_STEPS)
                    dve.wait_ge(acc_free, GROUPS[("out_b", i)] + 1)
                    g = gain[:, G_FFN + i:G_FFN + i + 1]
                    link(V.tensor_scalar(f_hi[:, i], h_sb[:, i], g, None, ALU.mult))
                    V.scalar_tensor_tensor(f_lo[:, i], h_sb[:, i], g, f_hi[:, i].bitcast(F32), ALU.mult,
                                           ALU.subtract).then_inc(h_split, 1)

            def gate_up(g, t, n_next):
                n = g * FGT + t
                dve.wait_ge(slot_done, NS + ff_slot(g, t, 0) + 1)
                V.tensor_tensor(gate_sb[:], acc[:, ff_bank(0)], rstd_h[:], ALU.mult).then_inc(acc_free, 1)
                split_ff(ff_slot(g, t, 2), 0, n_next)
                dve.wait_ge(slot_done, NS + ff_slot(g, t, 1) + 1)
                V.tensor_tensor(up_sb[:], acc[:, ff_bank(1)], rstd_h[:], ALU.mult).then_inc(acc_free, 1)
                dve.wait_ge(acc_free, NGROUPS + ff_slot(g, t, 1) + 1)
                dve.wait_ge(silu_done, n + 1)
                V.tensor_tensor(up_sb[:], up_sb[:], silu_sb[:], ALU.mult).then_inc(hid_made, 1)
                dve.wait_ge(hid_hi_done, n + 1)
                V.tensor_tensor(hid_lo[:, t], up_sb[:], hid_hi[:, t].bitcast(F32),
                                ALU.subtract).then_inc(hid_split, 1)
                split_ff(ff_slot(g, t, 3), 1, n_next)

            def down(g, t, n_next):
                for r in range(2):
                    dve.wait_ge(slot_done, NS + ff_slot(g, t + FGT, r) + 1)
                    V.tensor_tensor(h_sb[:, t * 2 + r], acc[:, ff_bank(r)], h_sb[:, t * 2 + r],
                                    ALU.add).then_inc(acc_free, 1)
                    if n_next:
                        split_ff(ff_slot(g, t + FGT, 2 + r), r, n_next)

            dve.wait_ge(rstd_done, NORM_AT["h"])
            ff_loops(dve, gate_up, down)

        @block.gpsimd
        def _(pool):
            G = nc.gpsimd
            chain = [0]

            def link(ins):
                chain[0] += 1
                ins.then_inc(pool_step, 1)
                pool.wait_ge(pool_step, chain[0])

            G.memset(ones[:], 1.0)
            G.memset(blk64[:], 1.0)
            G.memset(swap[:], 0.0)
            G.memset(ident[:], 0.0)
            G.memset(rep[:], 0.0)
            G.memset(eps, EPS)
            link(G.memset(causal[:], 0.0))
            link(G.affine_select(out=ident[:], in_=ident[:], compare_op=ALU.not_equal, fill=1.0, base=0,
                                 pattern=[[-1, P]], channel_multiplier=1))
            v = blk64[:].rearrange("p (b d) -> p b d", d=DA)
            link(G.affine_select(out=v, in_=v, compare_op=ALU.is_ge, fill=0.0, base=0,
                                 pattern=[[-DA, P // DA], [0, DA]], channel_multiplier=1))
            link(G.affine_select(out=v, in_=v, compare_op=ALU.is_ge, fill=0.0, base=DA - 1,
                                 pattern=[[DA, P // DA], [0, DA]], channel_multiplier=-1))
            v = rep[:].rearrange("p (h d) -> p h d", d=ROPE)
            link(G.affine_select(out=v, in_=v, compare_op=ALU.not_equal, fill=1.0, base=0,
                                 pattern=[[0, P // ROPE], [-1, ROPE]], channel_multiplier=1))
            half = ROPE // 2
            for j in range(P // half):
                v = swap[:, j * half:(j + 1) * half]
                G.affine_select(out=v, in_=v, compare_op=ALU.not_equal, fill=1.0 if j % 2 else -1.0,
                                base=-half * (j ^ 1), pattern=[[-1, half]], channel_multiplier=1)
            G.affine_select(out=causal[:, S - P:], in_=causal[:, S - P:], compare_op=ALU.is_ge, fill=-FILL, base=0,
                            pattern=[[-1, P]], channel_multiplier=1).then_inc(consts_made, 1)
            for c in range(0, KC, 2):
                pool.wait_ge(xsq_done, c + 1)
                if c == 0:
                    G.tensor_copy(xsum[:], x_sq[:, 0]).then_inc(xsum_done, 1)
                else:
                    pool.wait_ge(xsum_done, c // 2)
                    G.tensor_tensor(xsum[:], xsum[:], x_sq[:, c], ALU.add).then_inc(xsum_done, 1)
            for b in range(NB):
                pool.wait_ge(dist_made, b + 1)
                k0 = 0 if b else P
                if b:
                    link(G.affine_select(out=dist[:, b], in_=dist[:, b], compare_op=ALU.is_ge, fill=FILL, base=-1,
                                         pattern=[[1, 2 * P]], channel_multiplier=-1))
                G.affine_select(out=dist[:, b, k0:], in_=dist[:, b, k0:], compare_op=ALU.is_ge, fill=FILL,
                                base=P - k0, pattern=[[-1, 2 * P - k0]], channel_multiplier=1).then_inc(dist_masked, 1)
            for stage, i in plan:
                if stage == "swap":
                    x = k_rt[:] if i == 0 else q_rt[:, i - 1]
                    pool.wait_ge(swapped, i + 1)
                    pool.wait_ge(cos_made, 1)
                    link(G.tensor_tensor(x, x, cos[:], ALU.mult))
                    pool.wait_ge(swap_scaled, i + 1)
                    G.tensor_tensor(x, x, tmp[:] if i < 2 else pos_f[:], ALU.add).then_inc(rotated, 1)
                if stage != "sum":
                    continue
                name, k = i
                pool.wait_ge(sq_done, SQ_AT[i])
                src = sq[:, (SQ_AT[i] - 1) % 2]
                if k == 0:
                    pool.wait_ge(ss_done, SS_END[{"mem": "x", "c_q": "mem", "c_kv": "c_q"}[name]])
                    G.tensor_copy(xsum[:], src).then_inc(sum_done, 1)
                else:
                    pool.wait_ge(sum_done, SUM_AT[i] - 1)
                    G.tensor_tensor(xsum[:], xsum[:], src, ALU.add).then_inc(sum_done, 1)
            for m in range(KC):
                pool.wait_ge(hsq_done, m + 1)
                if m == 0:
                    G.tensor_copy(ssum[:], hsq[:, 0]).then_inc(hsum_done, 1)
                else:
                    pool.wait_ge(hsum_done, m)
                    G.tensor_tensor(ssum[:], ssum[:], hsq[:, m % 2], ALU.add).then_inc(hsum_done, 1)
            for m in range(KC // 2 - 1):
                last_t = ff_slot(FG - 1, FGT + m, 1)
                pool.wait_ge(acc_free, NGROUPS + last_t + 1)
                G.dma_start(outT[:, 2 * m:2 * m + 2], h_sb[:, 2 * m:2 * m + 2]).then_inc(out_sent, 16)
            pool.wait_ge(out_sent, 16 * (KC // 2 - 1))


def _tiles(w, n):
    k, m = w.shape
    return np.ascontiguousarray(w.reshape(k // P, P, m // n, n).transpose(2, 1, 0, 3)).reshape(m // n, P, k // P * n)


def _halves(w, n):
    k, m = w.shape
    return np.ascontiguousarray(
        w.reshape(2, k // P // 2, P, m // n, n).transpose(3, 0, 2, 1, 4)).reshape(m // n, 2, P, k // P // 2 * n)


def lay_out(i):
    col = lambda g: g.reshape(-1, P).T
    x, mem, pos = i["x"][0], i["mem"][0], i["positions"][0]
    w = i["w_in"][0]
    cuts = np.cumsum([0, HA * DA, GA * DA, GA * DA, RANK, RANK, ROPE, HM * P])
    wq, wk, wv, wcq, wckv, wkr, wqm = (w[:, a:b] for a, b in zip(cuts[:-1], cuts[1:]))
    wq = wq.reshape(D, GA, 8, DA).transpose(0, 2, 1, 3).reshape(D, HA * DA)
    big = np.concatenate([wk, wv, wq, wcq, wckv, wqm], axis=1)
    mkv = i["w_mem_kv"][0]
    uq = i["w_uq"][0].reshape(RANK, HB, NOPE + ROPE)
    uq = np.concatenate([uq[:, :, :NOPE].reshape(RANK, HB * NOPE),
                         uq[:, :, NOPE:].reshape(RANK, HB * ROPE)], axis=1)
    ukv = i["w_ukv"][0].reshape(RANK, HB, 2, P)
    wo = i["w_out"][0]
    wo_a = wo[:HA * DA].reshape(GA, 8, DA, D).transpose(1, 0, 2, 3).reshape(HA * DA, D)
    gu = np.stack([_tiles(i["w_gate"][0], P), _tiles(i["w_up"][0], P)], axis=1).reshape(2 * FT, P, KC * P)
    dn = i["w_down"][0].reshape(FG, FGT, P, KC, P).transpose(0, 3, 2, 1, 4)
    four = lambda g: np.tile(g, 4)[:, None]
    two = lambda g: np.tile(g, 2)[:, None]
    gains = np.concatenate([
        col(i["attn_norm_g"][0]), col(i["ffn_norm_g"][0]), col(i["mem_norm_g"][0]),
        two(i["swa_q_norm_g"][0]), two(i["swa_k_norm_g"][0]), col(i["mla_cq_norm_g"][0]),
        col(i["mla_ckv_norm_g"][0]), i["mla_qn_norm_g"][0][:, None], i["mla_kn_norm_g"][0][:, None],
        two(i["mla_qr_norm_g"][0]), two(i["mla_kr_norm_g"][0]),
        i["mem_q_norm_g"][0][:, None], i["mem_k_norm_g"][0][:, None]], axis=1)
    freq = (10000.0 ** (-np.arange(0, ROPE, 2, dtype=np.float32) / np.float32(ROPE))).astype(np.float32)
    chunks = lambda a: a.T.reshape(KC, P, -1).transpose(1, 0, 2)
    pairs = lambda t: t.reshape(t.shape[0] // 2, 2, P, -1).transpose(0, 2, 1, 3).reshape(t.shape[0] // 2, P, -1)
    vs = lambda w_, c, n: w_.reshape(-1, c, P, n).transpose(0, 2, 1, 3).reshape(-1, P, c * n)
    uv = ukv[:, :, 1].reshape(RANK, 2, 2 * P).transpose(1, 0, 2)
    return {
        "xT": chunks(x), "memT": chunks(mem), "pos_rows": np.broadcast_to(pos[None], (P, S)),
        "pos_cols": pos.reshape(NB, P).T, "gains": gains,
        "sink_rows": np.broadcast_to(i["swa_sinks"][0][None], (P, HA)), "inv_freq": four(freq),
        "w_in": _halves(big, P), "w_kr": _halves(wkr, ROPE)[0],
        "w_memk": _halves(mkv[:, :HM * P], P), "w_memv": vs(mkv[:, HM * P:], 2, HM * P),
        "w_uq": pairs(_tiles(uq, P)), "w_uk": pairs(_tiles(ukv[:, :, 0].reshape(RANK, HB * P), P)),
        "w_uv": np.stack([vs(uv[k], 4, 2 * P)[0] for k in range(2)]),
        "w_outa": _tiles(wo_a, P), "w_outb": _tiles(wo[HA * DA:], P),
        "w_gu": gu, "w_dn": dn.reshape(FG * KC, P, FGT * P),
    }


def kernel(**inputs):
    import concourse.bacc as bacc
    from concourse.bass_utils import run_bass_kernel_spmd

    nc = bacc.Bacc("TRN2", target_bir_lowering=False, num_devices=1)
    arrays = {k: np.ascontiguousarray(v) for k, v in lay_out({k: np.asarray(v) for k, v in inputs.items()}).items()}
    aps = {k: nc.dram_tensor(k, v.shape, mybir.dt.from_np(v.dtype), kind="ExternalInput").ap()
           for k, v in arrays.items()}
    outT = nc.dram_tensor("outT", (P, KC, S), F32, kind="ExternalOutput").ap()
    build_layer(nc, **aps, outT=outT)
    got = run_bass_kernel_spmd(nc, [arrays], core_ids=[0]).results[0]["outT"]
    return np.ascontiguousarray(got.transpose(2, 1, 0).reshape(1, S, D))
```
